# Optimizing a Trainium2 kernel written in Bass

```python
import jax, jax.numpy as jnp
from jax import lax
import numpy as np
import math

D_MODEL = 1024
BATCH = 1
SEQ = 1024
DEPTH = 2

GRID_W = 64
CTX_LEN = 256
HEAD_DIM = 64
ROPE_THETA = 10000.0
EPS = 1e-6
Q_BLOCK = 128
NEG_INF = -1e30
ATTN_SCALE = HEAD_DIM ** -0.5

A_HEADS = 8
A_KV_HEADS = 2
B_HEADS = 8
B_KV_HEADS = 2
B_WINDOW = 128
C_WIDTH = 512
C_CONV = 31
D_HEADS = 8
NA_KH = 8
NA_KW = 16

A_Q = A_HEADS * HEAD_DIM
A_KV = A_KV_HEADS * HEAD_DIM
B_Q = B_HEADS * HEAD_DIM
B_KV = B_KV_HEADS * HEAD_DIM
D_W = D_HEADS * HEAD_DIM
EVEN_WIDTHS = (A_Q, A_KV, A_KV, A_Q, B_Q, B_KV, B_KV, B_Q)
ODD_WIDTHS = (C_WIDTH, C_WIDTH, C_WIDTH, D_W, D_W, D_W, D_W)
EVEN_IN = sum(EVEN_WIDTHS)
ODD_IN = sum(ODD_WIDTHS)
EVEN_MIX = A_Q + B_Q
ODD_MIX = C_WIDTH + D_W


def rms_norm(x, g):
    xf = x.astype(jnp.float32)
    y = xf * lax.rsqrt(jnp.mean(xf * xf, axis=-1, keepdims=True) + EPS)
    return (y * g.astype(jnp.float32)).astype(x.dtype)

def layer_norm(x, g, b):
    xf = x.astype(jnp.float32)
    mu = jnp.mean(xf, axis=-1, keepdims=True)
    var = jnp.mean(jnp.square(xf - mu), axis=-1, keepdims=True)
    y = (xf - mu) * lax.rsqrt(var + EPS)
    return (y * g.astype(jnp.float32) + b.astype(jnp.float32)).astype(x.dtype)

def split_cols(h, widths):
    offs = [int(o) for o in np.cumsum(widths)[:-1]]
    return jnp.split(h, offs, axis=-1)

def heads(t, n_heads):
    return t.reshape(t.shape[:-1] + (n_heads, HEAD_DIM))

def group(q, kv_heads):
    return q.reshape(q.shape[:-2] + (kv_heads, q.shape[-2] // kv_heads, HEAD_DIM))

def axial_rope_tables(n):
    t = jnp.arange(n)
    row = (t // GRID_W).astype(jnp.float32)
    col = (t % GRID_W).astype(jnp.float32)
    half = HEAD_DIM // 2
    freqs = ROPE_THETA ** (-jnp.arange(0, half, 2, dtype=jnp.float32) / half)
    ang = jnp.concatenate([row[:, None] * freqs, col[:, None] * freqs], axis=-1)
    return jnp.cos(ang), jnp.sin(ang)

def apply_rope(x, cos, sin):
    xf = x.astype(jnp.float32)
    x1, x2 = xf[..., 0::2], xf[..., 1::2]
    c, s = cos[None, :, None, :], sin[None, :, None, :]
    out = jnp.stack([x1 * c - x2 * s, x1 * s + x2 * c], axis=-1).reshape(x.shape)
    return out.astype(x.dtype)

def gqa_attend(q, k, v, bias=None, sink=None):
    s = jnp.einsum("bqhgd,bkhd->bhgqk", q, k, preferred_element_type=jnp.float32) * ATTN_SCALE
    if bias is not None:
        s = s + bias
    if sink is not None:
        sink_col = jnp.broadcast_to(sink.astype(jnp.float32)[None, :, :, None, None], s.shape[:-1] + (1,))
        p = jax.nn.softmax(jnp.concatenate([s, sink_col], axis=-1), axis=-1)[..., :-1]
    else:
        p = jax.nn.softmax(s, axis=-1)
    return jnp.einsum("bhgqk,bkhd->bqhgd", p.astype(v.dtype), v)

def even_mixer(h_lat, h_ctx, w_in, w_out, q_gain, k_gain, sink, cos, sin, update_ctx):
    bsz, n, _ = h_lat.shape
    ctx_len = h_ctx.shape[1]
    n_blk = n // Q_BLOCK
    ga, gb = A_HEADS // A_KV_HEADS, B_HEADS // B_KV_HEADS
    sink = sink.reshape(B_KV_HEADS, gb)

    def project(h):
        aq, ak, av, ag, bq, bk, bv, bg = split_cols(h @ w_in, EVEN_WIDTHS)
        aq = rms_norm(heads(aq, A_HEADS), q_gain)
        ak = rms_norm(heads(ak, A_KV_HEADS), k_gain)
        return (aq, ak, heads(av, A_KV_HEADS), ag,
                heads(bq, B_HEADS), heads(bk, B_KV_HEADS), heads(bv, B_KV_HEADS), bg)

    aq, ak, av, ag, bq, bk, bv, bg = project(h_lat)
    c_aq, c_ak, c_av, c_ag, c_bq, c_bk, c_bv, c_bg = project(h_ctx)
    aq, ak, bq, bk = (apply_rope(t, cos, sin) for t in (aq, ak, bq, bk))

    ka = jnp.concatenate([c_ak, ak], axis=1)
    va = jnp.concatenate([c_av, av], axis=1)
    qa_blk = jnp.moveaxis(group(aq, A_KV_HEADS).reshape(bsz, n_blk, Q_BLOCK, A_KV_HEADS, ga, HEAD_DIM), 1, 0)
    oa = lax.map(lambda qb: gqa_attend(qb, ka, va), qa_blk)
    oa = jnp.moveaxis(oa, 0, 1).reshape(bsz, n, A_Q)

    band = Q_BLOCK + 2 * B_WINDOW
    kb_pad = jnp.pad(bk, ((0, 0), (B_WINDOW, B_WINDOW), (0, 0), (0, 0)))
    vb_pad = jnp.pad(bv, ((0, 0), (B_WINDOW, B_WINDOW), (0, 0), (0, 0)))
    rel = jnp.arange(band)[None, :] - B_WINDOW - jnp.arange(Q_BLOCK)[:, None]
    in_band = jnp.abs(rel) <= B_WINDOW
    ctx_open = jnp.zeros((Q_BLOCK, ctx_len), jnp.float32)
    qb_blk = jnp.moveaxis(group(bq, B_KV_HEADS).reshape(bsz, n_blk, Q_BLOCK, B_KV_HEADS, gb, HEAD_DIM), 1, 0)

    def b_block(args):
        blk, qb = args
        start = blk * Q_BLOCK
        kpos = start - B_WINDOW + jnp.arange(band)
        valid = in_band & ((kpos >= 0) & (kpos < n))[None, :]
        bias = jnp.concatenate([ctx_open, jnp.where(valid, 0.0, NEG_INF)], axis=-1)
        kk = jnp.concatenate([c_bk, lax.dynamic_slice_in_dim(kb_pad, start, band, axis=1)], axis=1)
        vv = jnp.concatenate([c_bv, lax.dynamic_slice_in_dim(vb_pad, start, band, axis=1)], axis=1)
        return gqa_attend(qb, kk, vv, bias, sink)

    ob = lax.map(b_block, (jnp.arange(n_blk), qb_blk))
    ob = jnp.moveaxis(ob, 0, 1).reshape(bsz, n, B_Q)

    y_lat = jnp.concatenate([oa * jax.nn.silu(ag), ob * jax.nn.silu(bg)], axis=-1) @ w_out
    if not update_ctx:
        return y_lat, None
    oa_c = gqa_attend(group(c_aq, A_KV_HEADS), c_ak, c_av).reshape(bsz, ctx_len, A_Q)
    ob_c = gqa_attend(group(c_bq, B_KV_HEADS), c_bk, c_bv, sink=sink).reshape(bsz, ctx_len, B_Q)
    y_ctx = jnp.concatenate([oa_c * jax.nn.silu(c_ag), ob_c * jax.nn.silu(c_bg)], axis=-1) @ w_out
    return y_lat, y_ctx

def conformer_conv(val, glu_gate, silu_gate, dw_w, dw_b, ln_g, ln_b):
    u = val * jax.nn.sigmoid(glu_gate)
    u = lax.conv_general_dilated(u, dw_w.reshape(C_CONV, 1, C_WIDTH), window_strides=(1,),
                                 padding=[(C_CONV // 2, C_CONV // 2)],
                                 dimension_numbers=("NWC", "WIO", "NWC"),
                                 feature_group_count=C_WIDTH) + dw_b
    u = jax.nn.silu(layer_norm(u, ln_g, ln_b))
    return u * jax.nn.silu(silu_gate)

def odd_mixer(h_lat, h_ctx, w_in, w_out, dw_w, dw_b, ln_g, ln_b, rpb, update_ctx):
    bsz, n, _ = h_lat.shape
    ctx_len = h_ctx.shape[1]
    rows = n // GRID_W
    kh = min(NA_KH, rows)

    cv, cgl, cg, dq, dk, dv, dg = split_cols(h_lat @ w_in, ODD_WIDTHS)
    x_cv, x_cgl, x_cg, x_dq, x_dk, x_dv, x_dg = split_cols(h_ctx @ w_in, ODD_WIDTHS)
    c_dk, c_dv = heads(x_dk, D_HEADS), heads(x_dv, D_HEADS)

    oc = conformer_conv(cv, cgl, cg, dw_w, dw_b, ln_g, ln_b)

    q_rows = jnp.moveaxis(heads(dq, D_HEADS).reshape(bsz, rows, GRID_W, D_HEADS, HEAD_DIM), 1, 0)
    k_grid = heads(dk, D_HEADS).reshape(bsz, rows, GRID_W, D_HEADS, HEAD_DIM)
    v_grid = heads(dv, D_HEADS).reshape(bsz, rows, GRID_W, D_HEADS, HEAD_DIM)
    cols = jnp.arange(GRID_W)
    col_start = jnp.clip(cols - NA_KW // 2, 0, GRID_W - NA_KW)
    col_in = (cols[None, :] >= col_start[:, None]) & (cols[None, :] < col_start[:, None] + NA_KW)
    col_mask = jnp.where(col_in, 0.0, NEG_INF)
    dc_idx = jnp.clip(cols[None, :] - cols[:, None] + NA_KW - 1, 0, 2 * NA_KW - 2)
    rpb = rpb.astype(jnp.float32)
    ctx_open = jnp.zeros((D_HEADS, GRID_W, ctx_len), jnp.float32)

    def d_row(args):
        r, qr = args
        rs = jnp.clip(r - kh // 2, 0, rows - kh)
        kr = lax.dynamic_slice_in_dim(k_grid, rs, kh, axis=1).reshape(bsz, kh * GRID_W, D_HEADS, HEAD_DIM)
        vr = lax.dynamic_slice_in_dim(v_grid, rs, kh, axis=1).reshape(bsz, kh * GRID_W, D_HEADS, HEAD_DIM)
        dr_idx = rs + jnp.arange(kh) - r + NA_KH - 1
        bias = rpb[:, dr_idx][:, :, dc_idx] + col_mask[None, None]
        bias = jnp.transpose(bias, (0, 2, 1, 3)).reshape(D_HEADS, GRID_W, kh * GRID_W)
        bias = jnp.concatenate([ctx_open, bias], axis=-1)[None, :, None]
        kk = jnp.concatenate([c_dk, kr], axis=1)
        vv = jnp.concatenate([c_dv, vr], axis=1)
        return gqa_attend(qr[:, :, :, None, :], kk, vv, bias).reshape(bsz, GRID_W, D_W)

    od = lax.map(d_row, (jnp.arange(rows), q_rows))
    od = jnp.moveaxis(od, 0, 1).reshape(bsz, n, D_W)

    y_lat = jnp.concatenate([oc, od * jax.nn.silu(dg)], axis=-1) @ w_out
    if not update_ctx:
        return y_lat, None
    oc_c = conformer_conv(x_cv, x_cgl, x_cg, dw_w, dw_b, ln_g, ln_b)
    od_c = gqa_attend(heads(x_dq, D_HEADS)[:, :, :, None, :], c_dk, c_dv).reshape(bsz, ctx_len, D_W)
    y_ctx = jnp.concatenate([oc_c, od_c * jax.nn.silu(x_dg)], axis=-1) @ w_out
    return y_lat, y_ctx

def modulation(cond, w, b):
    m = jax.nn.silu(cond) @ w + b
    return jnp.split(m, 3, axis=-1)

def first_inputs(seed: int = 0) -> dict:
    key = jax.random.key(seed)
    ks = jax.random.split(key, 24)
    n_even = (DEPTH + 1) // 2
    n_odd = DEPTH // 2
    f32 = jnp.float32

    def nrm(k, shape, scale):
        return jax.random.normal(k, shape, f32) * scale

    return {
        "x": nrm(ks[0], (BATCH, SEQ, D_MODEL), 1.0),
        "c": nrm(ks[1], (BATCH, D_MODEL), 1.0),
        "ctx": nrm(ks[2], (BATCH, CTX_LEN, D_MODEL), 1.0),
        "c_ctx": nrm(ks[3], (D_MODEL,), 1.0),
        "mod_w": nrm(ks[4], (DEPTH, D_MODEL, 3 * D_MODEL), 0.5 * D_MODEL ** -0.5),
        "mod_b": nrm(ks[5], (DEPTH, 3 * D_MODEL), 0.02),
        "norm_g": 1.0 + nrm(ks[6], (DEPTH, D_MODEL), 0.05),
        "ev_w_in": nrm(ks[7], (n_even, D_MODEL, EVEN_IN), D_MODEL ** -0.5),
        "ev_w_out": nrm(ks[8], (n_even, EVEN_MIX, D_MODEL), EVEN_MIX ** -0.5),
        "a_q_gain": 1.0 + nrm(ks[9], (n_even, HEAD_DIM), 0.05),
        "a_k_gain": 1.0 + nrm(ks[10], (n_even, HEAD_DIM), 0.05),
        "b_sink": nrm(ks[11], (n_even, B_HEADS), 0.5),
        "od_w_in": nrm(ks[12], (n_odd, D_MODEL, ODD_IN), D_MODEL ** -0.5),
        "od_w_out": nrm(ks[13], (n_odd, ODD_MIX, D_MODEL), ODD_MIX ** -0.5),
        "c_dw_w": nrm(ks[14], (n_odd, C_CONV, C_WIDTH), C_CONV ** -0.5),
        "c_dw_b": nrm(ks[15], (n_odd, C_WIDTH), 0.02),
        "c_ln_g": 1.0 + nrm(ks[16], (n_odd, C_WIDTH), 0.05),
        "c_ln_b": nrm(ks[17], (n_odd, C_WIDTH), 0.02),
        "d_rpb": nrm(ks[18], (n_odd, D_HEADS, 2 * NA_KH - 1, 2 * NA_KW - 1), 0.1),
        "final_g": 1.0 + nrm(ks[19], (D_MODEL,), 0.05),
    }

def first_block(x, c, ctx, c_ctx, mod_w, mod_b, norm_g, ev_w_in, ev_w_out, a_q_gain, a_k_gain, b_sink,
              od_w_in, od_w_out, c_dw_w, c_dw_b, c_ln_g, c_ln_b, d_rpb, final_g):
    n = x.shape[1]
    cos, sin = axial_rope_tables(n)
    x_lat, x_ctx = x, ctx
    for i in range(DEPTH):
        update_ctx = i < DEPTH - 1
        sh_l, sc_l, g_l = modulation(c, mod_w[i], mod_b[i])
        sh_c, sc_c, g_c = modulation(c_ctx, mod_w[i], mod_b[i])
        h_lat = rms_norm(x_lat, norm_g[i]) * (1.0 + sc_l[:, None, :]) + sh_l[:, None, :]
        h_ctx = rms_norm(x_ctx, norm_g[i]) * (1.0 + sc_c) + sh_c
        j = i // 2
        if i % 2 == 0:
            y_lat, y_ctx = even_mixer(h_lat, h_ctx, ev_w_in[j], ev_w_out[j], a_q_gain[j], a_k_gain[j],
                                      b_sink[j], cos, sin, update_ctx)
        else:
            y_lat, y_ctx = odd_mixer(h_lat, h_ctx, od_w_in[j], od_w_out[j], c_dw_w[j], c_dw_b[j],
                                     c_ln_g[j], c_ln_b[j], d_rpb[j], update_ctx)
        x_lat = x_lat + g_l[:, None, :] * y_lat
        if update_ctx:
            x_ctx = x_ctx + g_c * y_ctx
    return rms_norm(x_lat, final_g)


DEPTH_2 = 1

CHUNK = 64
N_MIXERS = 4
GLA_HEADS = 4
GLA_DK = (D_MODEL // 2) // GLA_HEADS
GLA_DV = D_MODEL // GLA_HEADS
GLA_GATE_RANK = 16
GLA_TAU = 16.0
GLA_IN = 2 * GLA_HEADS * GLA_DK + 2 * GLA_HEADS * GLA_DV + GLA_GATE_RANK
POOL_WINDOWS = (2, 4, 8, 16)
POOL_GROUPS = len(POOL_WINDOWS)
POOL_GW = D_MODEL // POOL_GROUPS
SSD_DINNER = 2 * D_MODEL
SSD_HEADDIM = 64
SSD_HEADS = SSD_DINNER // SSD_HEADDIM
SSD_GROUPS = 4
SSD_HPG = SSD_HEADS // SSD_GROUPS
SSD_STATE = 128
SSD_CONV = 4
SSD_CONV_DIM = SSD_DINNER + 2 * SSD_GROUPS * SSD_STATE
SSD_IN = SSD_DINNER + SSD_CONV_DIM + SSD_HEADS
SB_HEADS = 16
SB_HEADDIM = D_MODEL // SB_HEADS
SB_QBLOCK = 128
FFN_DIM = 2816
FFN_CONV = 3


def rms_normalize(x):
    xf = x.astype(jnp.float32)
    y = xf * lax.rsqrt(jnp.mean(xf * xf, axis=-1, keepdims=True) + EPS)
    return y.astype(x.dtype)

def rmsnorm(x, w):
    return rms_normalize(x) * w

def causal_dwconv(u, w, b):
    K = w.shape[0]
    L = u.shape[1]
    up = jnp.pad(u, ((0, 0), (K - 1, 0), (0, 0)))
    out = up[:, K - 1:K - 1 + L] * w[K - 1] + b
    for k in range(K - 1):
        out = out + up[:, k:k + L] * w[k]
    return out

def to_chunks(a):
    b_, l_ = a.shape[:2]
    return jnp.moveaxis(a.reshape(b_, l_ // CHUNK, CHUNK, *a.shape[2:]), 1, 0)

def from_chunks(a):
    a = jnp.moveaxis(a, 0, 1)
    return a.reshape(a.shape[0], a.shape[1] * a.shape[2], *a.shape[3:])

def gla_mixer(h, w_in, w_gate2, b_gate, norm_w, w_out):
    b_, l_, _ = h.shape
    hk, hv = GLA_HEADS * GLA_DK, GLA_HEADS * GLA_DV
    proj = h @ w_in
    q, k, v, r, glr = jnp.split(proj, [hk, 2 * hk, 2 * hk + hv, 2 * hk + 2 * hv], axis=-1)
    q = q.reshape(b_, l_, GLA_HEADS, GLA_DK).astype(jnp.float32) * (GLA_DK ** -0.5)
    k = k.reshape(b_, l_, GLA_HEADS, GLA_DK).astype(jnp.float32)
    v = v.reshape(b_, l_, GLA_HEADS, GLA_DV).astype(jnp.float32)
    log_a = jax.nn.log_sigmoid((glr @ w_gate2 + b_gate).astype(jnp.float32)) / GLA_TAU
    log_a = log_a.reshape(b_, l_, GLA_HEADS, GLA_DK)
    qc, kc, vc, lac = to_chunks(q), to_chunks(k), to_chunks(v), to_chunks(log_a)
    g = jnp.cumsum(lac, axis=2)
    g_end = g[:, :, -1]
    k_dec = kc * jnp.exp(g_end[:, :, None] - g)

    def body(state, inp):
        q_c, kd_c, v_c, ge_c = inp
        state = state * jnp.exp(ge_c)[..., None] + jnp.einsum('bshk,bshv->bhkv', kd_c, v_c)
        o = jnp.einsum('bqhk,bhkv->bqhv', q_c, state)
        return state, o

    s0 = jnp.zeros((b_, GLA_HEADS, GLA_DK, GLA_DV), jnp.float32)
    _, o = lax.scan(body, s0, (qc, k_dec, vc, g_end))
    o = rms_normalize(from_chunks(o)).reshape(b_, l_, hv) * norm_w
    o = o.astype(h.dtype) * jax.nn.silu(r)
    return o @ w_out

def pool_mixer(h, w_grp, b_grp, scale):
    b_, l_, d_ = h.shape
    hf = h.astype(jnp.float32)
    cs = jnp.concatenate([jnp.zeros((b_, 1, d_), jnp.float32), jnp.cumsum(hf, axis=1)], axis=1)
    t1 = jnp.arange(1, l_ + 1, dtype=jnp.float32)
    outs = []
    for gi, win in enumerate(POOL_WINDOWS):
        sl = slice(gi * POOL_GW, (gi + 1) * POOL_GW)
        c = cs[..., sl]
        lower = jnp.concatenate([jnp.zeros((b_, win - 1, POOL_GW), jnp.float32), c[:, :l_ + 1 - win]], axis=1)
        mean = (c[:, 1:] - lower) / jnp.minimum(t1, float(win))[None, :, None]
        dlt = (mean - hf[..., sl]).astype(h.dtype)
        outs.append(dlt @ w_grp[gi] + b_grp[gi])
    return jnp.concatenate(outs, axis=-1) * scale

def ssd_mixer(h, w_in, conv_w, conv_b, dt_bias, a_log, d_skip, norm_w, w_out):
    b_, l_, _ = h.shape
    G, HG, P, N = SSD_GROUPS, SSD_HPG, SSD_HEADDIM, SSD_STATE
    proj = h @ w_in
    z, xbc, dt = jnp.split(proj, [SSD_DINNER, SSD_DINNER + SSD_CONV_DIM], axis=-1)
    xbc = jax.nn.silu(causal_dwconv(xbc, conv_w, conv_b))
    xs, bm, cm = jnp.split(xbc, [SSD_DINNER, SSD_DINNER + G * N], axis=-1)
    xs = xs.reshape(b_, l_, G, HG, P)
    bm = bm.reshape(b_, l_, G, N)
    cm = cm.reshape(b_, l_, G, N)
    dt = jax.nn.softplus((dt + dt_bias).astype(jnp.float32)).reshape(b_, l_, G, HG)
    a_h = -jnp.exp(a_log.astype(jnp.float32)).reshape(G, HG)
    causal = jnp.tril(jnp.ones((CHUNK, CHUNK), bool))

    def body(state, inp):
        x_c, b_c, c_c, dt_c = inp
        acs = jnp.cumsum(dt_c * a_h, axis=1)
        seg = acs[:, :, None] - acs[:, None, :]
        lmat = jnp.exp(jnp.where(causal[None, :, :, None, None], seg, -jnp.inf))
        xdt = x_c * dt_c[..., None]
        cb = jnp.einsum('btgn,bsgn->btsg', c_c, b_c)
        y = jnp.einsum('btsg,btsgh,bsghp->btghp', cb, lmat, xdt)
        y = y + jnp.einsum('btgn,bghpn,btgh->btghp', c_c, state, jnp.exp(acs))
        decay_end = jnp.exp(acs[:, -1:] - acs)
        state = state * jnp.exp(acs[:, -1])[..., None, None] + jnp.einsum('bsgn,bsgh,bsghp->bghpn', b_c, decay_end, xdt)
        return state, y

    s0 = jnp.zeros((b_, G, HG, P, N), jnp.float32)
    _, ys = lax.scan(body, s0, (to_chunks(xs), to_chunks(bm), to_chunks(cm), to_chunks(dt)))
    y = from_chunks(ys) + d_skip.reshape(G, HG)[..., None] * xs
    y = y.reshape(b_, l_, SSD_DINNER) * jax.nn.silu(z)
    y = rms_normalize(y.reshape(b_, l_, G, SSD_DINNER // G)).reshape(b_, l_, SSD_DINNER) * norm_w
    return y.astype(h.dtype) @ w_out

def sb_mixer(h, w_qkv, w_out):
    b_, l_, _ = h.shape
    q, k, v = jnp.split(h @ w_qkv, 3, axis=-1)
    q = q.reshape(b_, l_, SB_HEADS, SB_HEADDIM).transpose(0, 2, 1, 3) * (SB_HEADDIM ** -0.5)
    k = k.reshape(b_, l_, SB_HEADS, SB_HEADDIM).transpose(0, 2, 1, 3)
    v = v.reshape(b_, l_, SB_HEADS, SB_HEADDIM).transpose(0, 2, 1, 3)
    nb = l_ // SB_QBLOCK
    qb = jnp.moveaxis(q.reshape(b_, SB_HEADS, nb, SB_QBLOCK, SB_HEADDIM), 2, 0)
    starts = jnp.arange(nb, dtype=jnp.int32) * SB_QBLOCK
    key_pos = jnp.arange(l_, dtype=jnp.int32)

    def block(inp):
        q_i, start = inp
        zt = jnp.einsum('bhqd,bhkd->bhqk', q_i, k).astype(jnp.float32)
        qpos = start + jnp.arange(SB_QBLOCK, dtype=jnp.int32)
        mask = key_pos[None, :] < qpos[:, None]
        log_1mb = jnp.where(mask, jax.nn.log_sigmoid(-zt), 0.0)
        rc = lax.cumsum(log_1mb, axis=3, reverse=True)
        surv = jnp.concatenate([rc[..., 1:], jnp.zeros_like(rc[..., :1])], axis=-1)
        att = jnp.where(mask, jnp.exp(jax.nn.log_sigmoid(zt) + surv), 0.0)
        return jnp.einsum('bhqk,bhkd->bhqd', att.astype(v.dtype), v)

    o = lax.map(block, (qb, starts))
    o = jnp.moveaxis(o, 0, 2).reshape(b_, SB_HEADS, l_, SB_HEADDIM)
    o = o.transpose(0, 2, 1, 3).reshape(b_, l_, D_MODEL)
    return o @ w_out

def conv_ffn(h, w_up, conv_w, conv_b, w_down):
    u = causal_dwconv(h @ w_up, conv_w, conv_b)
    g, val = jnp.split(u, 2, axis=-1)
    return (jax.nn.silu(g) * val) @ w_down

def second_inputs(seed: int = 0) -> dict:
    key = jax.random.key(seed)
    ks = list(jax.random.split(key, 40))
    f32 = jnp.float32

    def nrm(i, shape, scale):
        return jax.random.normal(ks[i], shape, f32) * scale

    n_a = len(range(0, DEPTH_2, N_MIXERS))
    n_b = len(range(1, DEPTH_2, N_MIXERS))
    n_c = len(range(2, DEPTH_2, N_MIXERS))
    n_d = len(range(3, DEPTH_2, N_MIXERS))
    dt0 = jnp.exp(jax.random.uniform(ks[20], (n_c, SSD_HEADS), f32) * (math.log(0.1) - math.log(0.001)) + math.log(0.001))
    return {
        'x': nrm(0, (BATCH, SEQ, D_MODEL), 1.0),
        'mix_norm_w': 1.0 + nrm(1, (DEPTH_2, D_MODEL), 0.02),
        'ffn_norm_w': 1.0 + nrm(2, (DEPTH_2, D_MODEL), 0.02),
        'final_norm_w': 1.0 + nrm(3, (D_MODEL,), 0.02),
        'gla_w_in': nrm(4, (n_a, D_MODEL, GLA_IN), D_MODEL ** -0.5),
        'gla_w_gate2': nrm(5, (n_a, GLA_GATE_RANK, GLA_HEADS * GLA_DK), GLA_GATE_RANK ** -0.5),
        'gla_b_gate': nrm(6, (n_a, GLA_HEADS * GLA_DK), 0.1),
        'gla_norm_w': 1.0 + nrm(7, (n_a, GLA_HEADS * GLA_DV), 0.02),
        'gla_w_out': nrm(8, (n_a, GLA_HEADS * GLA_DV, D_MODEL), (GLA_HEADS * GLA_DV) ** -0.5),
        'pool_w': nrm(9, (n_b, POOL_GROUPS, POOL_GW, POOL_GW), POOL_GW ** -0.5),
        'pool_b': nrm(10, (n_b, POOL_GROUPS, POOL_GW), 0.02),
        'pool_scale': 1.0 + nrm(11, (n_b, D_MODEL), 0.02),
        'ssd_w_in': nrm(12, (n_c, D_MODEL, SSD_IN), D_MODEL ** -0.5),
        'ssd_conv_w': nrm(13, (n_c, SSD_CONV, SSD_CONV_DIM), SSD_CONV ** -0.5),
        'ssd_conv_b': nrm(14, (n_c, SSD_CONV_DIM), 0.02),
        'ssd_dt_bias': dt0 + jnp.log(-jnp.expm1(-dt0)),
        'ssd_a_log': jnp.log(jax.random.uniform(ks[15], (n_c, SSD_HEADS), f32, 1.0, 16.0)),
        'ssd_d': 1.0 + nrm(16, (n_c, SSD_HEADS), 0.02),
        'ssd_norm_w': 1.0 + nrm(17, (n_c, SSD_DINNER), 0.02),
        'ssd_w_out': nrm(18, (n_c, SSD_DINNER, D_MODEL), SSD_DINNER ** -0.5),
        'sb_w_qkv': nrm(19, (n_d, D_MODEL, 3 * D_MODEL), D_MODEL ** -0.5),
        'sb_w_out': nrm(21, (n_d, D_MODEL, D_MODEL), D_MODEL ** -0.5),
        'ffn_w_up': nrm(22, (DEPTH_2, D_MODEL, 2 * FFN_DIM), D_MODEL ** -0.5),
        'ffn_conv_w': nrm(23, (DEPTH_2, FFN_CONV, 2 * FFN_DIM), FFN_CONV ** -0.5),
        'ffn_conv_b': nrm(24, (DEPTH_2, 2 * FFN_DIM), 0.02),
        'ffn_w_down': nrm(25, (DEPTH_2, FFN_DIM, D_MODEL), FFN_DIM ** -0.5),
    }

def second_block(x, mix_norm_w, ffn_norm_w, final_norm_w,
              gla_w_in, gla_w_gate2, gla_b_gate, gla_norm_w, gla_w_out,
              pool_w, pool_b, pool_scale,
              ssd_w_in, ssd_conv_w, ssd_conv_b, ssd_dt_bias, ssd_a_log, ssd_d, ssd_norm_w, ssd_w_out,
              sb_w_qkv, sb_w_out,
              ffn_w_up, ffn_conv_w, ffn_conv_b, ffn_w_down):
    for i in range(DEPTH_2):
        m, j = i % N_MIXERS, i // N_MIXERS
        h = rmsnorm(x, mix_norm_w[i])
        if m == 0:
            y = gla_mixer(h, gla_w_in[j], gla_w_gate2[j], gla_b_gate[j], gla_norm_w[j], gla_w_out[j])
        elif m == 1:
            y = pool_mixer(h, pool_w[j], pool_b[j], pool_scale[j])
        elif m == 2:
            y = ssd_mixer(h, ssd_w_in[j], ssd_conv_w[j], ssd_conv_b[j], ssd_dt_bias[j], ssd_a_log[j],
                          ssd_d[j], ssd_norm_w[j], ssd_w_out[j])
        else:
            y = sb_mixer(h, sb_w_qkv[j], sb_w_out[j])
        x = x + y.astype(x.dtype)
        h = rmsnorm(x, ffn_norm_w[i])
        x = x + conv_ffn(h, ffn_w_up[i], ffn_conv_w[i], ffn_conv_b[i], ffn_w_down[i]).astype(x.dtype)
    return rmsnorm(x, final_norm_w)


def setup_inputs(seed=0):
    out = dict(first_inputs(seed))
    for name, value in second_inputs(seed + 1).items():
        if name != "x":
            out[name + "_2"] = value
    return out


def reference(
    x, c, ctx, c_ctx, mod_w, mod_b, norm_g, ev_w_in, ev_w_out, a_q_gain, a_k_gain, b_sink,
    od_w_in, od_w_out, c_dw_w, c_dw_b, c_ln_g, c_ln_b, d_rpb, final_g, mix_norm_w_2,
    ffn_norm_w_2, final_norm_w_2, gla_w_in_2, gla_w_gate2_2, gla_b_gate_2, gla_norm_w_2,
    gla_w_out_2, pool_w_2, pool_b_2, pool_scale_2, ssd_w_in_2, ssd_conv_w_2, ssd_conv_b_2,
    ssd_dt_bias_2, ssd_a_log_2, ssd_d_2, ssd_norm_w_2, ssd_w_out_2, sb_w_qkv_2, sb_w_out_2,
    ffn_w_up_2, ffn_conv_w_2, ffn_conv_b_2, ffn_w_down_2,
):
    x = first_block(
        x, c, ctx, c_ctx, mod_w, mod_b, norm_g, ev_w_in, ev_w_out, a_q_gain, a_k_gain, b_sink,
        od_w_in, od_w_out, c_dw_w, c_dw_b, c_ln_g, c_ln_b, d_rpb, final_g,
    )
    return second_block(
        x, mix_norm_w_2, ffn_norm_w_2, final_norm_w_2, gla_w_in_2, gla_w_gate2_2, gla_b_gate_2,
        gla_norm_w_2, gla_w_out_2, pool_w_2, pool_b_2, pool_scale_2, ssd_w_in_2, ssd_conv_w_2,
        ssd_conv_b_2, ssd_dt_bias_2, ssd_a_log_2, ssd_d_2, ssd_norm_w_2, ssd_w_out_2,
        sb_w_qkv_2, sb_w_out_2, ffn_w_up_2, ffn_conv_w_2, ffn_conv_b_2, ffn_w_down_2,
    )


_drawn_inputs = setup_inputs


def setup_inputs(seed=0):
    import zlib

    import numpy as np

    out = dict(_drawn_inputs(seed))
    spreads = {}
    factors = {'mod_b': 3.976,
     'norm_g': 5.072,
     'a_q_gain': 8.0,
     'a_k_gain': 8.0,
     'b_sink': 8.0,
     'c_dw_b': 8.0,
     'c_ln_g': 7.54,
     'c_ln_b': 8.0,
     'd_rpb': 8.0,
     'ffn_norm_w_2': 4.266,
     'final_norm_w_2': 2.838,
     'gla_norm_w_2': 4.95,
     'ffn_conv_b_2': 4.321}
    for name, (base, spread) in spreads.items():
        noise = np.random.default_rng([zlib.crc32(name.encode()), seed]).standard_normal(out[name].shape)
        drawn = base * np.exp(spread * noise) if base else spread * noise
        out[name] = __import__('jax').numpy.asarray(drawn.astype(out[name].dtype))
    for name, factor in factors.items():
        out[name] = (out[name] * factor).astype(out[name].dtype)
    return out
```

```python
from contextlib import ExitStack

import concourse.bass as bass
from concourse import mybir
from concourse.alu_op_type import AluOpType as ALU

ACT = mybir.ActivationFunctionType
F32 = mybir.dt.float32
AX_X = mybir.AxisListType.X

P = 128
LAT, CTX, D = 1024, 256, 1024
TOK = LAT + CTX
KT = D // P
BANK = 512
SLOT = 3 * BANK
HEADS, DH, QT = 8, 64, LAT // P
EPS = 1e-6
WSLOTS = 4
UP_T, DOWN_K = 44, 22
GH, GDV, CHUNK, NCH = 4, 256, 64, LAT // 64
CONV = 31
PAD = CONV // 2
GRID = 64
D_LOCAL = 10 * GRID
D_BASE = [min(max(2 * j - 4, 0), 6) for j in range(QT)]
D_CLASS = [0, 1, 2, 2, 2, 2, 3, 4]

STREAM = [("mod0", 24), ("evA", 10), ("mod1", 24), ("evB", 10), ("evO", 8), ("od", 28), ("odO", 8),
          ("gla", 24), ("glaO", 8), ("up", UP_T)]
GBASE, NW = {}, 0
for _n, _c in STREAM:
    GBASE[_n] = NW
    NW += _c

VEC = [("c", 16), ("mod_b", 48), ("norm_g", 16), ("q_gain", 1), ("k_gain", 1), ("sink", 8), ("conv_w", 4 * CONV),
       ("conv_b", 4), ("ln_g", 4), ("ln_b", 4), ("final_g", 8), ("mix_g", 8), ("ffn_g", 8), ("out_g", 8),
       ("gate_b", 4), ("gla_g", 8), ("ffn_w", 3 * UP_T), ("ffn_b", UP_T)]
VOFF, NV = {}, 0
for _n, _c in VEC:
    VOFF[_n] = NV
    NV += _c


RPB_ROWS, RPB_PAD = 20, 64


def RPB_AT(h, e):
    return RPB_PAD + (h * RPB_ROWS + e) * 31 + 15


def product_tiles():
    out = [("mod0", "mod", 0), ("n0", "nrm", 0)]
    for ph in ("evA", "evB"):
        for m in range(5):
            out.append((ph, "qk", m))
            if ph == "evA" and m >= 1:
                out.append((ph, "ssq", m - 1))
        out += [(ph, "v", i) for i in range(TOK // P)]
        if ph == "evA":
            out.append((ph, "ssq", 4))
        out += [(ph, "gate", m) for m in range(4)]
    out += [("evO", "res", m) for m in range(KT)]
    out += [("n1", "nrm", 0)]
    for j in range(4):
        out += [("od", "cgl", j), ("od", "cv", j)]
    out += [("od", "v", i) for i in range(TOK // P)]
    out += [("od", "cg", j) for j in range(4)]
    out += [("od", "dq", j) for j in range(4)]
    out += [("od", "dk", j) for j in range(4)]
    out += [("od", "dg", j) for j in range(4)]
    out += [("od", "lnm", 0), ("od", "lnv", 0)]
    out += [("odO", "res", m) for m in range(KT)]
    out += [("n2", "nrm", 0), ("n3", "nrm", 0)]
    out += [("gla", "k", m) for m in range(4)] + [("gla", "glr", 0)]
    for m in range(4):
        out += [("gla", "z", m)] + [("gla", "v", 4 * m + i) for i in range(4)]
    out += [("gla", "q", m) for m in range(4)]
    out += [("gla", "r", m) for m in range(8)]
    out += [("glaN", "ssq", h) for h in range(GH)]
    out += [("glaO", "res", m) for m in range(KT)]
    out += [("n4", "nrm", 0)]
    out += [("up", "up", m) for m in range(UP_T)]
    out += [("down", "res", m) for m in range(KT)]
    out += [("n5", "nrm", 0)]
    return out


TILES = product_tiles()
TINDEX = {key: t for t, key in enumerate(TILES)}


def attention_plan(units, heads_per_group, mods=0):
    n = len(units)
    groups = n // heads_per_group
    steps, tg, done_mods = [], 0, 0
    for s in range(n + 6):
        st = {"S": s if s < n else None, "T": [], "PV": s - 3 if 0 <= s - 3 < n else None,
              "NORM": None, "OT": None, "MOD": None, "X": s - 1 if 0 <= s - 1 < n else None}
        u = s - 2
        if 0 <= u < n:
            nt = units[u]["nt"]
            for i, j in enumerate(range(0, nt, 4)):
                st["T"].append((tg, u, j, min(4, nt - j), "act" if i else "dve"))
                tg += 1
        v = s - 4
        if 0 <= v < n and v % heads_per_group == heads_per_group - 1:
            st["NORM"] = v // heads_per_group
            st["OT"] = (tg, v // heads_per_group)
            tg += 1
        if mods and s % heads_per_group == 5 and done_mods < mods:
            st["MOD"] = (tg, done_mods)
            tg += 1
            done_mods += 3
        steps.append(st)
    assert done_mods == mods and groups * heads_per_group == n
    return steps


def program(nc, wall, wdown, wglr, wgate2, vec, xl_in, xc_in, consts, ropes, bmask, dmask, rpb, out):
    with ExitStack() as ctx:
        def sb(name, shape):
            return ctx.enter_context(nc.sbuf_tensor(name, shape, F32))

        def sem(name):
            return ctx.enter_context(nc.semaphore(name))

        XL = sb("x_lat", [P, KT, LAT])
        XC = sb("x_ctx", [P, KT * CTX])
        XCv = XC[:, :].rearrange("p (k n) -> p k n", k=KT)
        CST = sb("consts", [P, 3 * P])
        IDENT, ONES, BONES = CST[:, 0:P], CST[:, P:2 * P], CST[:, 2 * P:3 * P]
        V = sb("vectors", [P, NV])
        SC = sb("silu_c", [P, KT, 2])
        MOD = sb("modulation", [P, 2, 24, 2])
        MA = sb("mod_scale", [P, 2, KT, 2])
        GQ = sb("q_gain_scaled", [P, 1])
        ST = sb("softmax_stats", [P, 2, 4, 8])
        DEC = sb("chunk_decay", [P, GH, NCH])
        NSINK = sb("negated_sink", [P, HEADS])
        MODRAW = sb("modulation_raw", [P, 24, 2])
        ARENA = 41760
        A = sb("arena", [P, ARENA])
        expanded = nc.dram_tensor("expanded_bias", (HEADS, RPB_ROWS, GRID, GRID), F32, kind="Internal").ap()
        ps = ctx.enter_context(nc.psum_tensor("ps", [P, 8 * BANK], F32))

        def area(off, *shape):
            n = 1
            for x in shape:
                n *= x
            assert off + n <= ARENA, (off, n)
            v = A[:, off:off + n]
            if len(shape) == 2:
                v = v.rearrange("p (a b) -> p a b", a=shape[0])
            return v

        def vcol(name, i=0, n=1):
            return V[:, VOFF[name] + i:VOFF[name] + i + n]

        W = area(0, WSLOTS, KT * P).rearrange("p s (k m) -> p s k m", k=KT)
        H = area(4096, KT, TOK)
        QK = area(14336, 5, TOK)
        VE = area(20736, TOK // P, P)
        G = area(22016, KT, TOK)
        ROPE = area(32256, 2, LAT)
        SCR = 34304
        SQ = area(SCR, 2, TOK)
        RS = area(SCR + 2 * TOK, TOK)
        SW = area(SCR + 3 * TOK, LAT)
        U = area(14336, 4, LAT + 2 * PAD)
        CG = area(18552, 4, LAT)
        DQ = area(22648, 4, LAT)
        DK = area(26744, 4, TOK)
        DV = area(31864, TOK // P, 512)
        DG = area(36984, 4, LAT)
        BT = area(4096, 2, HEADS * D_LOCAL)
        HG = area(4096, KT, LAT)
        GQT = area(12288, 4, LAT)
        GKT = area(16384, 4, LAT)
        GV = area(20480, QT, D)
        GR = area(28672, KT, LAT)
        GLR = area(36864, LAT)
        SMASK = area(37888, LAT)
        S01 = area(38912, 2, LAT)
        STATE = area(40960, 2, GDV)
        ACTV = area(12288, DOWN_K, LAT)
        FACC = area(34816, 4, LAT)
        WD = [area(38912, DOWN_K, P), area(0, DOWN_K, P)]
        SG = area(36984, LAT)
        ZERO = area(41080, CTX)
        GSMALL_2 = XC[0:16, 0:512]
        GSMALL_W = XC[:, 512:512 + KT * 16]
        GSMALL_Wv = GSMALL_W.rearrange("p (k m) -> p k m", k=KT)

        def NSQ(ph, k):
            return {"n0": SQ, "n1": SQ, "n2": area(14336, 2, LAT), "n3": area(14336, 2, LAT),
                    "n4": area(12288, 2, LAT), "n5": area(4096, 2, LAT)}[ph][:, k % 2, :]

        def NRS(ph):
            return {"n0": RS, "n1": RS, "n2": area(18552, LAT), "n3": area(18552, LAT), "n4": area(14336, LAT),
                    "n5": area(6144, LAT)}[ph]

        def up_ffn(m):
            return m // 2 + (m % 2) * DOWN_K

        w_in = [sem(f"weights_in_slot{i}") for i in range(WSLOTS)]
        w_mod = sem("mod_weights_used")
        ps_ready = sem("product_ready")
        ps_free = [sem(f"product_slot{i}_free") for i in range(2)]
        dve_done = sem("dve_step")
        act_done = sem("act_step")
        pool_done = sem("pool_step")
        loads = sem("first_loads")
        rope_in = sem("rope_in")
        table_in = sem("bias_table_expanded")
        small_in = sem("gla_small_in")
        bmask_in = sem("band_mask_in")
        dmask_in = [sem(f"grid_mask_in{i}") for i in range(2)]
        bias_in = [sem(f"bias_rows_in{i}") for i in range(2)]
        bias_ready = sem("bias_ready")
        down_in = [sem(f"down_weights_in{i}") for i in range(2)]
        silu_c = sem("silu_c_ready")
        mod_ready = sem("modulation_ready")
        x_done = sem("residual_written")
        sq_ready = sem("squares_ready")
        sq_used = sem("squares_summed")
        ms_ready = sem("mean_square_ready")
        sd_ready = sem("root_ready")
        hn = sem("normed_ready")
        h_ready = sem("h_ready")
        qk_done = sem("qk_ready")
        g_ready = sem("act_tiles_ready")
        v_ready = sem("v_ready")
        outs = sem("outputs_written")
        raw_ready = sem("raw_evacuated")
        u_zero = sem("pads_zeroed")
        sig_ready = sem("sigmoid_ready")
        u_done = sem("conv_inputs_ready")
        conv_done = sem("conv_ready")
        ln_sub = sem("centred_ready")
        ln_mul = sem("ln_scaled")
        ln_act = sem("ln_silu_ready")
        mix_ready = sem("conv_mix_ready")
        glr_ready = sem("glr_ready")
        zb_ready = sem("z_ready")
        sp_ready = sem("softplus_ready")
        gc_ready = sem("gate_sums_ready")
        ge_ready = sem("gate_exps_ready")
        kd_ready = sem("decayed_k_ready")
        kt_ready = sem("k_transposed")
        kt_free = sem("k_t_evacuated")
        kv_ready = sem("chunk_kv_ready")
        st_ready = sem("state_ready")
        o_ready = sem("chunk_out_ready")
        oe_ready = sem("gla_out_evacuated")
        gm_ready = sem("gla_mix_ready")
        fa_ready = sem("ffn_conv_started")
        fc_ready = sem("ffn_conv_ready")
        fs_ready = sem("ffn_silu_ready")
        fm_ready = sem("ffn_product_ready")

        def slot(t):
            return (t % 2) * SLOT

        def tile(ph, kind, i=0):
            t = TINDEX[(ph, kind, i)]
            return t, slot(t)

        NORM_CTX = ("n0", "n1")
        X_BASE = {"n1": 0, "n2": 8, "n4": 16, "n5": 24}
        G_BASE = {"cg": 10, "od_end": 26, "gla_end": 58}
        H_READY_OUT = 40
        SQU_BASE, b = {}, 0
        for name, n in [("n0", 7), ("n1", 7), ("ln", 3), ("n2", 7), ("n3", 7), ("glaN", 4), ("n4", 7), ("n5", 7)]:
            SQU_BASE[name] = b
            b += n
        SQ_BASE, HN_BASE, H_BASE = {}, {}, {}
        sq_order = [("n0", 8), ("evA", 5), ("n1", 8), ("ln", 4), ("n2", 8), ("n3", 8), ("glaN", 8), ("n4", 8), ("n5", 8)]
        b = 0
        for name, n in sq_order:
            SQ_BASE[name] = b
            b += n
        ms_order = [("n0", 1), ("evA", 5), ("n1", 1), ("ln", 1), ("n2", 1), ("n3", 1), ("glaN", 4), ("n4", 1), ("n5", 1)]
        MS_BASE, b = {}, 0
        for name, n in ms_order:
            MS_BASE[name] = b
            b += n

        scale_q = DH ** -0.5
        def unit_a(qt, h, ctx_q):
            hp = 64 * (h // 4)
            qcol = (LAT if ctx_q else 0) + qt * P
            u = {"h": h, "q": QK[hp:hp + 64, h % 4, qcol:qcol + P]}
            vs = slice(64 * (h // 4), 64 * (h // 4) + 64)
            if ctx_q:
                u["chunks"] = [(0, QK[hp:hp + 64, 4, LAT:TOK], CTX)]
                u["v"] = [VE[:, QT + i, vs] for i in range(2)]
                u["span"] = (0, CTX)
            else:
                u["chunks"] = [(c, QK[hp:hp + 64, 4, c:c + n], n) for c, n in ((0, 512), (512, 512), (LAT, CTX))]
                u["v"] = [VE[:, i, vs] for i in range(TOK // P)]
                u["span"] = (0, TOK)
            u["mask"] = None
            u["nt"] = len(u["v"])
            u["gate"] = (qcol, qcol + P)
            return u

        BM = area(SCR + 4 * 640 + BANK, 1152)

        def unit_b(qt, h, ctx_q):
            u = unit_a(qt, h, ctx_q)
            if not ctx_q:
                hp = 64 * (h // 4)
                vs = slice(64 * (h // 4), 64 * (h // 4) + 64)
                lo, hi = max(qt - 1, 0), min(qt + 2, QT)
                w = (hi - lo) * P
                u["chunks"] = [(BANK - w, QK[hp:hp + 64, 4, lo * P:hi * P], w),
                               (BANK, QK[hp:hp + 64, 4, LAT:TOK], CTX)]
                u["span"] = (BANK - w, BANK + CTX)
                u["v"] = [VE[:, i, vs] for i in list(range(lo, hi)) + [QT, QT + 1]]
                u["nt"] = len(u["v"])
                u["mask"] = BM[:, 640:1152] if qt == QT - 1 else BM[:, (128 if qt == 0 else 0):640]
            return u

        def unit_d(qt, h):
            hp = 64 * (h % 2)
            b0 = D_BASE[qt] * GRID
            u = {"h": h, "q": DQ[hp:hp + 64, h // 2, qt * P:(qt + 1) * P]}
            kk = DK[hp:hp + 64, h // 2, :]
            u["chunks"] = [(0, DK[hp:hp + 64, h // 2, b0:b0 + 512], 512),
                           (512, DK[hp:hp + 64, h // 2, b0 + 512:b0 + 640], 128),
                           (640, DK[hp:hp + 64, h // 2, LAT:TOK], CTX)]
            u["span"] = (0, D_LOCAL + CTX)
            u["v"] = [DV[:, i, h * 64:(h + 1) * 64] for i in list(range(b0 // P, b0 // P + 5)) + [QT, QT + 1]]
            u["nt"] = 7
            u["mask"] = "grid"
            u["gate"] = (qt * P, (qt + 1) * P)
            return u

        att_units = {
            "A": [unit_a(q, h, False) for q in range(QT) for h in range(HEADS)]
            + [unit_a(q, h, True) for q in range(2) for h in range(HEADS)],
            "B": [unit_b(q, h, False) for q in range(QT) for h in range(HEADS)]
            + [unit_b(q, h, True) for q in range(2) for h in range(HEADS)],
            "D": [unit_d(q, h) for q in range(QT) for h in range(HEADS)],
        }
        att = {}
        for name, units in att_units.items():
            width = {"A": TOK, "B": 640, "D": D_LOCAL + CTX}[name]
            base = SCR if name != "D" else 14336
            at = {"units": units, "plan": attention_plan(units, HEADS, 24 if name == "A" else 0),
                  "P": area(base, 2, width), "PT": area(base + 2 * width, 2, width),
                  "ON": area(base + 4 * width, BANK),
                  "gate": (lambda a, b: G[:, 0:4, a:b]) if name == "A" else
                          (lambda a, b: G[:, 4:8, a:b]) if name == "B" else
                          (lambda a, b: DG[:, :, a:b]),
                  "sink": name == "B"}
            at["tb"] = [6 * BANK] if name == "A" else [6 * BANK, 2 * BANK]
            at["t_free"] = [sem(f"att{name}_t_free{i}") for i in range(len(at["tb"]))]
            for s in ("scores", "maxed", "exped", "t_ready", "pv", "normed", "sink_in", "sink_out", "mixed"):
                at[s] = sem(f"att{name}_{s}")
            att[name] = at
        TB, OB = 6 * BANK, 7 * BANK

        def tbank(at, tg):
            return at["tb"][tg % len(at["tb"])]

        def tfree(at, tg):
            nb = len(at["tb"])
            return at["t_free"][tg % nb], tg // nb + 1

        def tgs(at, u):
            return [x for st in at["plan"] for x in st["T"] if x[1] == u]

        def weights_done(g):
            ph = next(n for n, c in STREAM if GBASE[n] <= g < GBASE[n] + c)
            i = g - GBASE[ph]
            if ph == "mod0":
                return w_mod, i + 1
            if ph == "mod1":
                tg = next(st["MOD"][0] for st in att["A"]["plan"] if st["MOD"] and st["MOD"][1] == 3 * (i // 3))
                return att["A"]["t_ready"], tg + 1
            if ph in ("evA", "evB"):
                key = (ph, "qk", i) if i < 5 else (ph, "v", TOK // P - 1) if i == 5 else (ph, "gate", i - 6)
            elif ph == "od":
                key = ((ph, "cgl" if i % 2 == 0 else "cv", i // 2) if i < 8 else (ph, "v", TOK // P - 1) if i < 12 else
                       (ph, ("cg", "dq", "dk", "dg")[(i - 12) // 4], i % 4))
            elif ph == "gla":
                key = ((ph, "k", i) if i < 4 else (ph, "v", QT - 1) if i < 8 else (ph, "v", 2 * QT - 1) if i < 12 else
                       (ph, "q", i - 12) if i < 16 else (ph, "r", i - 16))
            elif ph == "up":
                key = (ph, "up", i)
            else:
                key = (ph, "res", i)
            return ps_ready, TINDEX[key] + 1

        block = ctx.enter_context(nc.Block())

        @block.sync
        def _(sp):
            for dst, src in ((V[:, :], vec), (CST[:, :], consts)):
                sp.dma_start(dst, src).then_inc(loads, 16)

            def load_weight(g):
                if g >= WSLOTS:
                    s, v = weights_done(g - WSLOTS)
                    sp.wait_ge(s, v)
                sp.dma_start(A[:, (g % WSLOTS) * 1024:(g % WSLOTS + 1) * 1024], wall[g]).then_inc(w_in[g % WSLOTS], 16)

            for g in range(WSLOTS):
                load_weight(g)
            sp.dma_start(XL[:, :, :], xl_in).then_inc(loads, 16)
            sp.dma_start(XCv, xc_in).then_inc(loads, 16)
            sp.dma_start(ROPE, ropes).then_inc(rope_in, 16)
            for g in range(WSLOTS, NW):
                if g == GBASE["evO"]:
                    sp.wait_ge(qk_done, 10)
                    sp.dma_start(BM, bmask).then_inc(bmask_in, 16)
                load_weight(g)
            for m in range(KT):
                if m == 0:
                    sp.wait_ge(gm_ready, 8)
                    sp.wait_ge(ps_ready, TINDEX[("glaO", "res", 0)] + 1)
                if m == 1:
                    sp.wait_ge(ps_ready, TINDEX[("up", "up", UP_T - 1)] + 1)
                if m >= 2:
                    sp.wait_ge(ps_ready, TINDEX[("down", "res", m - 2)] + 1)
                sp.dma_start(WD[m % 2], wdown[m].rearrange("p (k m) -> p k m", k=DOWN_K)).then_inc(down_in[m % 2], 16)
            for k in range(KT):
                sp.wait_ge(h_ready, H_READY_OUT + k + 1)
                sp.dma_start(out[:, k, :], XL[:, k, :]).then_inc(outs, 16)
            sp.wait_ge(outs, 16 * KT)

        @block.gpsimd
        def _(pool):
            src = bass.AP(rpb.tensor, RPB_AT(0, 0), [[31, HEADS * RPB_ROWS], [-1, GRID], [1, GRID]])
            pool.dma_start(expanded.rearrange("h r q k -> (h r) q k"), src).then_inc(table_in, 16)
            pool.wait_ge(att["B"]["mixed"], 10)
            pool.memset(U[:, :, 0:PAD], 0.0).then_inc(u_zero, 1)
            pool.memset(U[:, :, PAD + LAT:LAT + 2 * PAD], 0.0).then_inc(u_zero, 1)

            def bias(cls):
                s = cls % 2
                qt = D_CLASS.index(cls)
                if cls == 0:
                    pool.wait_ge(table_in, 16)
                    pool.wait_ge(ps_ready, TINDEX[("od", "dg", 3)] + 1)
                    pool.wait_ge(mix_ready, 4)
                if cls >= 2:
                    last = max(i for i in range(QT) if D_CLASS[i] == cls - 2)
                    pool.wait_ge(att["D"]["maxed"], (last + 1) * HEADS)
                for half in range(2):
                    e = D_BASE[qt] - 2 * qt - half + 7 + 2
                    for h in range(HEADS):
                        dst = BT[64 * half:64 * half + 64, s, h * D_LOCAL:(h + 1) * D_LOCAL].rearrange("p (r c) -> p r c", r=10)
                        src = expanded[h, e:e + 10].rearrange("r q k -> q r k")
                        pool.dma_start(dst, src).then_inc(bias_in[s], 16)
                pool.dma_start(XC[:, s * D_LOCAL:(s + 1) * D_LOCAL], dmask[cls]).then_inc(dmask_in[s], 16)
                pool.wait_ge(bias_in[s], 16 * 16 * (cls // 2 + 1))
                pool.wait_ge(dmask_in[s], 16 * (cls // 2 + 1))
                for h in range(HEADS):
                    dst = BT[:, s, h * D_LOCAL:(h + 1) * D_LOCAL]
                    pool.tensor_tensor(dst, dst, XC[:, s * D_LOCAL:(s + 1) * D_LOCAL], ALU.add).then_inc(bias_ready, 1)

            for cls in range(5):
                bias(cls)
            pool.wait_ge(ps_ready, TINDEX[("odO", "res", KT - 1)] + 1)
            pool.memset(SMASK, 1.0).then_inc(pool_done, 1)
            pool.wait_ge(pool_done, 1)
            pool.memset(SMASK.rearrange("p (c s) -> p c s", s=CHUNK)[:, :, 0:1], 0.0).then_inc(pool_done, 1)
            pool.wait_ge(bias_ready, 5 * HEADS)
            pool.dma_start(GSMALL_W, wglr).then_inc(small_in, 16)
            pool.dma_start(GSMALL_2, wgate2).then_inc(small_in, 16)

        @block.tensor
        def _(pe):
            def wait_slot(t):
                if t >= 2:
                    pe.wait_ge(ps_free[t % 2], t // 2)

            def wait_weight(g):
                pe.wait_ge(w_in[g % WSLOTS], 16 * (g // WSLOTS + 1))

            def product(key, g, rhs, chunks, k_ready=None):
                t, o = tile(*key)
                wait_weight(g)
                wait_slot(t)
                for k in range(KT):
                    if k_ready:
                        pe.wait_ge(*k_ready(k))
                    for c, n in chunks:
                        mm = pe.matmul(ps[:, o + c:o + c + n], W[:, g % WSLOTS, k, :], rhs(k, c, n),
                                       start=(k == 0), stop=(k == KT - 1))
                mm.then_inc(ps_ready, 1)

            full = ((0, 512), (512, 512), (LAT, CTX))
            lat = ((0, 512), (512, 512))

            def hrow(k, c, n):
                return H[:, k, c:c + n]

            def norm_sums(ph):
                t, o = tile(ph, "nrm")
                wait_slot(t)
                for k in range(KT):
                    pe.wait_ge(sq_ready, SQ_BASE[ph] + k + 1)
                    for c, n in (full if ph in NORM_CTX else lat):
                        mm = pe.matmul(ps[:, o + c:o + c + n], ONES, NSQ(ph, k)[:, c:c + n], start=(k == 0), stop=(k == KT - 1))
                    if k < KT - 1:
                        mm.then_inc(sq_used, 1)
                mm.then_inc(ps_ready, 1)

            def group_sums(ph, i, mat, parts, chunks, o, sqs):
                for j in range(parts):
                    for c, n in chunks:
                        mm = pe.matmul(ps[:, o + c:o + c + n], mat, sqs(j)[:, c:c + n], start=(j == 0), stop=(j == parts - 1))
                return mm

            pe.wait_ge(loads, 64)
            pe.wait_ge(silu_c, 1)
            t, o = tile("mod0", "mod")
            for m in range(24):
                wait_weight(m)
                for k in range(KT):
                    mm = pe.matmul(ps[:, o + 2 * m:o + 2 * m + 2], W[:, m % WSLOTS, k, :], SC[:, k, :],
                                   start=(k == 0), stop=(k == KT - 1))
                mm.then_inc(w_mod, 1)
            pe.wait_ge(w_mod, 24)
            pe.nop().then_inc(ps_ready, 1)
            norm_sums("n0")

            def even_half(ph, first):
                g0 = GBASE[ph]
                def ssq(m):
                    t, o = tile(ph, "ssq", m)
                    wait_slot(t)
                    pe.wait_ge(sq_ready, SQ_BASE["evA"] + m + 1)
                    for c, n in full:
                        mm = pe.matmul(ps[:, o + c:o + c + n], BONES, SQ[:, m % 2, c:c + n], start=True, stop=True)
                    mm.then_inc(ps_ready, 1)

                for m in range(5):
                    product((ph, "qk", m), g0 + m, hrow, full, (lambda k: (h_ready, k + 1)) if first and m == 0 else None)
                    if first and m >= 1:
                        ssq(m - 1)
                wait_weight(g0 + 5)
                for i in range(TOK // P):
                    t, o = tile(ph, "v", i)
                    wait_slot(t)
                    for k in range(KT):
                        mm = pe.matmul(ps[:, o:o + P], H[:, k, i * P:(i + 1) * P], W[:, (g0 + 5) % WSLOTS, k, :],
                                       start=(k == 0), stop=(k == KT - 1))
                    mm.then_inc(ps_ready, 1)
                if first:
                    ssq(4)
                for m in range(4):
                    product((ph, "gate", m), g0 + 6 + m, hrow, full)

            def attention(name, t_next):
                at = att[name]
                units = at["units"]
                for s in range(2):
                    pe.wait_ge(ps_free[s], (t_next + 1 - s) // 2)
                for st in at["plan"]:
                    def scores(i):
                        u = units[st["S"]]
                        c, k, n = u["chunks"][i]
                        o = (st["S"] % 2) * SLOT
                        if i == 0 and st["S"] >= 2:
                            pe.wait_ge(at["exped"], st["S"] - 1)
                        mm = pe.matmul(ps[:, o + c:o + c + n], u["q"], k, start=True, stop=True)
                        if i == len(u["chunks"]) - 1:
                            mm.then_inc(at["scores"], 1)

                    def wait_bank(tg):
                        if tg >= len(at["tb"]):
                            pe.wait_ge(*tfree(at, tg - len(at["tb"])))
                        return tbank(at, tg)

                    def transposes(i):
                        tg, u, j, n, _ = st["T"][i]
                        if i == 0:
                            pe.wait_ge(at["exped"], u + 1)
                        tb = wait_bank(tg)
                        for x in range(n):
                            mm = pe.transpose(ps[:, tb + x * P:tb + (x + 1) * P],
                                              at["P"][:, u % 2, (j + x) * P:(j + x + 1) * P], IDENT)
                        mm.then_inc(at["t_ready"], 1)

                    def values(j0, j1):
                        v = st["PV"]
                        u = units[v]
                        if j0 == 0:
                            for x in tgs(at, v):
                                pe.wait_ge(*tfree(at, x[0]))
                            if v % HEADS == 0 and v:
                                pe.wait_ge(at["normed"], v // HEADS)
                        for j in range(j0, j1):
                            mm = pe.matmul(ps[:, OB + u["h"] * 64:OB + u["h"] * 64 + 64],
                                           at["PT"][:, v % 2, j * P:(j + 1) * P], u["v"][j], start=(j == 0), stop=(j == u["nt"] - 1))
                        if j1 == u["nt"]:
                            mm.then_inc(at["pv"], 1)

                    ns = len(units[st["S"]]["chunks"]) if st["S"] is not None else 0
                    nt = units[st["PV"]]["nt"] if st["PV"] is not None else 0
                    for i in range(max(ns, 2)):
                        if i < ns:
                            scores(i)
                        if i < min(len(st["T"]), 2):
                            transposes(i)
                    if nt:
                        values(0, nt // 2)
                    if len(st["T"]) > 2:
                        transposes(2)
                    if st["OT"]:
                        tg, g = st["OT"]
                        pe.wait_ge(at["normed"], g + 1)
                        tb = wait_bank(tg)
                        for x in range(4):
                            mm = pe.transpose(ps[:, tb + x * P:tb + (x + 1) * P], at["ON"][:, x * P:(x + 1) * P], IDENT)
                        mm.then_inc(at["t_ready"], 1)
                    if st["MOD"]:
                        tg, m0 = st["MOD"]
                        tb = wait_bank(tg)
                        for m in range(m0, m0 + 3):
                            g = GBASE["mod1"] + m
                            wait_weight(g)
                            for k in range(KT):
                                mm = pe.matmul(ps[:, tb + 2 * (m - m0):tb + 2 * (m - m0) + 2], W[:, g % WSLOTS, k, :], SC[:, k, :],
                                               start=(k == 0), stop=(k == KT - 1))
                        mm.then_inc(at["t_ready"], 1)
                    if nt:
                        values(nt // 2, nt)

            even_half("evA", True)
            pe.wait_ge(qk_done, 5)
            pe.wait_ge(v_ready, 10)
            attention("A", TINDEX[("evB", "qk", 0)])
            pe.wait_ge(att["A"]["exped"], len(att["A"]["units"]))
            pe.wait_ge(att["A"]["mixed"], 10)
            even_half("evB", False)
            pe.wait_ge(qk_done, 10)
            pe.wait_ge(v_ready, 20)
            attention("B", TINDEX[("evO", "res", 0)])
            pe.wait_ge(att["B"]["mixed"], 10)
            for m in range(KT):
                product(("evO", "res", m), GBASE["evO"] + m, lambda k, c, n: G[:, k, c:c + n], full)
            norm_sums("n1")

            g0 = GBASE["od"]
            for j in range(4):
                for x, kind in enumerate(("cgl", "cv")):
                    first = j == 0 and x == 0
                    product(("od", kind, j), g0 + 2 * j + x, hrow, lat, (lambda k: (h_ready, 8 + k + 1)) if first else None)
            for i in range(4):
                wait_weight(g0 + 8 + i)
            for i in range(TOK // P):
                t, o = tile("od", "v", i)
                wait_slot(t)
                for k in range(KT):
                    mm = pe.matmul(ps[:, o:o + 512], H[:, k, i * P:(i + 1) * P], W[:, :, k, :],
                                   start=(k == 0), stop=(k == KT - 1))
                mm.then_inc(ps_ready, 1)
            for x, kind in enumerate(("cg", "dq", "dk", "dg")):
                for j in range(4):
                    product(("od", kind, j), g0 + 12 + 4 * x + j, hrow, full if kind == "dk" else lat)
            t, o = tile("od", "lnm")
            wait_slot(t)
            for j in range(4):
                pe.wait_ge(conv_done, j + 1)
                for c, n in lat:
                    mm = pe.matmul(ps[:, o + c:o + c + n], ONES, U[:, j, PAD + c:PAD + c + n], start=(j == 0), stop=(j == 3))
            mm.then_inc(ps_ready, 1)
            t, o = tile("od", "lnv")
            wait_slot(t)
            for j in range(4):
                pe.wait_ge(sq_ready, SQ_BASE["ln"] + j + 1)
                for c, n in lat:
                    mm = pe.matmul(ps[:, o + c:o + c + n], ONES, XC[:, c:c + n], start=(j == 0), stop=(j == 3))
                if j < 3:
                    mm.then_inc(sq_used, 1)
            mm.then_inc(ps_ready, 1)
            pe.wait_ge(g_ready, G_BASE["od_end"])
            attention("D", TINDEX[("odO", "res", 0)])
            pe.wait_ge(att["D"]["mixed"], QT)
            pe.wait_ge(mix_ready, 4)
            for m in range(KT):
                product(("odO", "res", m), GBASE["odO"] + m,
                        lambda k, c, n: CG[:, k, c:c + n] if k < 4 else DG[:, k - 4, c:c + n], lat)
            norm_sums("n2")
            norm_sums("n3")

            def hg(k, c, n):
                return HG[:, k, c:c + n]

            g0 = GBASE["gla"]
            for m in range(4):
                product(("gla", "k", m), g0 + m, hg, lat, (lambda k: (h_ready, 24 + k + 1)) if m == 0 else None)
            pe.wait_ge(small_in, 32)
            t, o = tile("gla", "glr")
            wait_slot(t)
            for k in range(KT):
                for c, n in lat:
                    mm = pe.matmul(ps[0:16, o + c:o + c + n], GSMALL_Wv[:, k, :], HG[:, k, c:c + n], start=(k == 0), stop=(k == KT - 1))
            mm.then_inc(ps_ready, 1)
            pe.wait_ge(glr_ready, 1)
            for m in range(4):
                t, o = tile("gla", "z", m)
                wait_slot(t)
                for c, n in lat:
                    mm = pe.matmul(ps[:, o + c:o + c + n], GSMALL_2[:, m * P:(m + 1) * P], GLR[0:16, c:c + n], start=True, stop=True)
                mm.then_inc(ps_ready, 1)
                if m % 2 == 0:
                    for i in range(4):
                        wait_weight(g0 + 4 + 2 * m + i)
                for n in range(4 * m, 4 * m + 4):
                    i = n % QT
                    t, o = tile("gla", "v", n)
                    wait_slot(t)
                    for k in range(KT):
                        mm = pe.matmul(ps[:, o:o + 512], HG[:, k, i * P:(i + 1) * P], W[:, :, k, :],
                                       start=(k == 0), stop=(k == KT - 1))
                    mm.then_inc(ps_ready, 1)
            for m in range(4):
                product(("gla", "q", m), g0 + 12 + m, hg, lat)
            for m in range(8):
                product(("gla", "r", m), g0 + 16 + m, hg, lat)
            for h in range(GH):
                pe.wait_ge(kd_ready, h + 1)
                if h:
                    pe.wait_ge(kt_free, h)
                for i in range(QT):
                    mm = pe.transpose(ps[:, TB + i * P:TB + (i + 1) * P], GKT[:, h, i * P:(i + 1) * P], IDENT)
                mm.then_inc(kt_ready, 1)
            tn = TINDEX[("glaN", "ssq", 0)]
            for s in range(2):
                pe.wait_ge(ps_free[s], (tn + 1 - s) // 2)
            pe.wait_ge(kt_free, GH)
            pe.wait_ge(g_ready, G_BASE["gla_end"])
            steps = GH * NCH

            def kv(i):
                h, c = divmod(i, NCH)
                r = 64 * (c % 2)
                if i >= 4:
                    pe.wait_ge(st_ready, i - 3)
                pe.matmul(ps[:, (i % 4) * BANK:(i % 4) * BANK + GDV], GKT[r:r + 64, h, (c // 2) * P:(c // 2 + 1) * P],
                          GV[r:r + 64, c // 2, h * GDV:(h + 1) * GDV], start=True, stop=True).then_inc(kv_ready, 1)

            def chunk_out(i):
                h, c = divmod(i, NCH)
                b = 4 + 2 * (c // 8)
                pe.wait_ge(st_ready, i + 1)
                if c % 8 == 0 and i >= NCH:
                    pe.wait_ge(oe_ready, 2 * (2 * (h - 1) + c // 8) + 2)
                for half in range(2):
                    col = (b + half) * BANK + (c % 8) * CHUNK
                    mm = pe.matmul(ps[:, col:col + CHUNK], STATE[:, i % 2, half * P:(half + 1) * P],
                                   GQT[:, h, c * CHUNK:(c + 1) * CHUNK], start=True, stop=True)
                mm.then_inc(o_ready, 1)

            kv(0)
            kv(1)
            for i in range(steps):
                if i + 2 < steps:
                    kv(i + 2)
                chunk_out(i)
            for h in range(GH):
                t, o = tile("glaN", "ssq", h)
                wait_slot(t)
                for j in range(2):
                    pe.wait_ge(sq_ready, SQ_BASE["glaN"] + 2 * h + j + 1)
                    for c, n in lat:
                        mm = pe.matmul(ps[:, o + c:o + c + n], ONES, S01[:, 0, c:c + n], start=(j == 0), stop=(j == 1))
                    if j == 0:
                        mm.then_inc(sq_used, 1)
                mm.then_inc(ps_ready, 1)
            pe.wait_ge(gm_ready, 8)
            for m in range(KT):
                product(("glaO", "res", m), GBASE["glaO"] + m, lambda k, c, n: GR[:, k, c:c + n], lat)
            norm_sums("n4")
            for m in range(UP_T):
                product(("up", "up", m), GBASE["up"] + m, hg, lat, (lambda k: (h_ready, 32 + k + 1)) if m == 0 else None)
            for m in range(KT):
                t, o = tile("down", "res", m)
                pe.wait_ge(down_in[m % 2], 16 * (m // 2 + 1))
                wait_slot(t)
                for k in range(DOWN_K):
                    if m == 0:
                        pe.wait_ge(fm_ready, k + 1)
                    for c, n in lat:
                        mm = pe.matmul(ps[:, o + c:o + c + n], WD[m % 2][:, k, :], ACTV[:, k, c:c + n],
                                       start=(k == 0), stop=(k == DOWN_K - 1))
                mm.then_inc(ps_ready, 1)
            norm_sums("n5")

        @block.scalar
        def _(act):
            count = [0]

            def link(ins):
                count[0] += 1
                ins.then_inc(act_done, 1)
                act.wait_ge(act_done, count[0])

            def ready(ph, kind, i=0):
                t, o = tile(ph, kind, i)
                act.wait_ge(ps_ready, t + 1)
                return t, o

            used = [0]

            def squares(ph):
                for k in range(KT):
                    if ph in X_BASE:
                        act.wait_ge(x_done, X_BASE[ph] + k + 1)
                    if ph == "n3":
                        act.wait_ge(h_ready, 16 + k + 1)
                    if k >= 2:
                        act.wait_ge(sq_used, SQU_BASE[ph] + k - 1)
                    if ph in NORM_CTX:
                        act.activation(NSQ(ph, k)[:, LAT:TOK], XCv[:, k, :], ACT.Square)
                    act.activation(NSQ(ph, k)[:, 0:LAT], XL[:, k, :], ACT.Square).then_inc(sq_ready, 1)

            def root(name, i, rs):
                act.wait_ge(ms_ready, MS_BASE[name] + i + 1)
                act.activation(rs, rs, ACT.Sqrt).then_inc(sd_ready, 1)

            def modulate(layer, base):
                for k in range(KT):
                    act.wait_ge(hn, base + k + 1)
                    act.activation(H[:, k, LAT:TOK], H[:, k, LAT:TOK], ACT.Identity, bias=MOD[:, layer, k, 1:2],
                                   scale=MA[:, layer, k, 1:2])
                    act.activation(H[:, k, 0:LAT], H[:, k, 0:LAT], ACT.Identity, bias=MOD[:, layer, k, 0:1],
                                   scale=MA[:, layer, k, 0:1]).then_inc(h_ready, 1)

            act.wait_ge(loads, 64)
            act.activation(SC[:, :, :], vcol("c", 0, 16).rearrange("p (k a) -> p k a", a=2), ACT.Silu).then_inc(silu_c, 1)
            squares("n0")
            root("n0", 0, NRS("n0"))
            act.wait_ge(mod_ready, 1)
            modulate(0, 0)

            def even_half(ph, first):
                for m in range(5):
                    t, o = ready(ph, "qk", m)
                    if first:
                        if m >= 2:
                            act.wait_ge(ps_ready, TINDEX[(ph, "ssq", m - 2)] + 1)
                        act.activation(QK[:, m, :], ps[:, o:o + TOK], ACT.Copy)
                        act.activation(SQ[:, m % 2, :], ps[:, o:o + TOK], ACT.Square).then_inc(sq_ready, 1)
                        act.wait_ge(sq_ready, SQ_BASE["evA"] + m + 1)
                        act.nop().then_inc(ps_free[t % 2], 1)
                        if m >= 1:
                            root("evA", m - 1, RS)
                    else:
                        act.activation(QK[:, m, :], ps[:, o:o + TOK], ACT.Copy,
                                       scale=scale_q if m < 4 else 1.0).then_inc(ps_free[t % 2], 1)
                        act.wait_ge(ps_free[t % 2], t // 2 + 1)
                        act.nop().then_inc(raw_ready, 1)
                if first:
                    root("evA", 4, RS)
                for m in range(4):
                    t, o = ready(ph, "gate", m)
                    act.activation(G[:, (0 if first else 4) + m, :], ps[:, o:o + TOK], ACT.Silu).then_inc(ps_free[t % 2], 1)

            def attention(name):
                at = att[name]
                units = at["units"]
                for st in at["plan"]:
                    if st["X"] is not None:
                        u = st["X"]
                        c0, c1 = units[u]["span"]
                        o = (u % 2) * SLOT
                        act.wait_ge(at["maxed"], u + 1)
                        masked = units[u]["mask"] is not None
                        if u >= 2 and not masked:
                            act.wait_ge(at["t_ready"], tgs(at, u - 2)[-1][0] + 1)
                        src = at["P"][:, u % 2, 0:c1 - c0] if masked else ps[:, o + c0:o + c1]
                        g, h = divmod(u, HEADS)
                        act.activation(at["P"][:, u % 2, 0:c1 - c0], src, ACT.Exp, bias=ST[:, g % 2, 1, h:h + 1],
                                       accum_out=ST[:, g % 2, 2, h:h + 1]).then_inc(at["exped"], 1)
                        if at["sink"] and h == HEADS - 1:
                            act.wait_ge(at["sink_in"], g + 1)
                            act.activation(ST[:, g % 2, 3, :], ST[:, g % 2, 3, :], ACT.Exp).then_inc(at["sink_out"], 1)
                    for tg, u, j, n, eng in st["T"]:
                        if eng == "act":
                            act.wait_ge(at["t_ready"], tg + 1)
                            act.activation(at["PT"][:, u % 2, j * P:(j + n) * P], ps[:, tbank(at, tg):tbank(at, tg) + n * P], ACT.Copy)\
                               .then_inc(tfree(at, tg)[0], 1)

            even_half("evA", True)
            attention("A")
            even_half("evB", False)
            attention("B")
            squares("n1")
            root("n1", 0, NRS("n1"))
            act.wait_ge(mod_ready, 2)
            modulate(1, 8)

            for j in range(4):
                t, o = ready("od", "cgl", j)
                if j:
                    act.wait_ge(u_done, j)
                act.activation(SG, ps[:, o:o + LAT], ACT.Sigmoid).then_inc(sig_ready, 1)
                act.wait_ge(sig_ready, j + 1)
                act.nop().then_inc(ps_free[t % 2], 1)
            def evac(key, dst, n, func=ACT.Copy, scale=1.0):
                t, o = ready(*key)
                act.activation(dst, ps[:, o:o + n], func, scale=scale).then_inc(ps_free[t % 2], 1)
                act.wait_ge(ps_free[t % 2], t // 2 + 1)
                act.nop().then_inc(g_ready, 1)
            for i in range(TOK // P):
                if i == 0:
                    act.wait_ge(u_done, 4)
                evac(("od", "v", i), DV[:, i, :], 512)
            for j in range(4):
                evac(("od", "cg", j), CG[:, j, :], LAT, ACT.Silu)
            for j in range(4):
                evac(("od", "dq", j), DQ[:, j, :], LAT, ACT.Copy, scale_q)
            for j in range(4):
                evac(("od", "dk", j), DK[:, j, :], TOK)
            for j in range(4):
                evac(("od", "dg", j), DG[:, j, :], LAT, ACT.Silu)
            for j in range(4):
                act.wait_ge(ln_sub, j + 1)
                if j:
                    act.wait_ge(sq_used, SQU_BASE["ln"] + j)
                act.activation(XC[:, 0:LAT], U[:, j, PAD:PAD + LAT], ACT.Square).then_inc(sq_ready, 1)
            root("ln", 0, XC[:, LAT:2 * LAT])
            for j in range(4):
                act.wait_ge(ln_mul, j + 1)
                act.activation(U[:, j, PAD:PAD + LAT], U[:, j, PAD:PAD + LAT], ACT.Silu, bias=vcol("ln_b", j),
                               scale=vcol("ln_g", j)).then_inc(ln_act, 1)
            act.wait_ge(mix_ready, 4)
            attention("D")
            squares("n2")
            root("n2", 0, NRS("n2"))
            squares("n3")
            root("n3", 0, NRS("n3"))

            for m in range(4):
                evac(("gla", "k", m), GKT[:, m, :], LAT)
            t, o = ready("gla", "glr")
            act.activation(GLR[0:16, :], ps[0:16, o:o + LAT], ACT.Copy).then_inc(ps_free[t % 2], 1)
            act.wait_ge(ps_free[t % 2], t // 2 + 1)
            act.nop().then_inc(glr_ready, 1)

            def gate_chain(m):
                act.wait_ge(zb_ready, m + 1)
                link(act.activation(S01[:, 1, :], S01[:, 0, :], ACT.Abs))
                link(act.activation(S01[:, 1, :], S01[:, 1, :], ACT.Exp, scale=-1.0))
                act.activation(S01[:, 1, :], S01[:, 1, :], ACT.Ln, bias=1.0).then_inc(sp_ready, 1)
                act.wait_ge(gc_ready, m + 1)
                act.activation(DEC[:, m, :], S01[:, 0, :].rearrange("p (c s) -> p c s", s=CHUNK)[:, :, CHUNK - 1], ACT.Exp,
                               scale=1.0 / 16)
                act.activation(S01[:, 1, :], S01[:, 1, :], ACT.Exp, scale=1.0 / 16).then_inc(ge_ready, 1)

            for m in range(4):
                gate_chain(m)
                for i in range(4):
                    n = 4 * m + i
                    evac(("gla", "v", n), GV[:, n % QT, (n // QT) * 512:(n // QT + 1) * 512], 512)
            for m in range(4):
                evac(("gla", "q", m), GQT[:, m, :], LAT, ACT.Copy, 128 ** -0.5)
            for m in range(8):
                evac(("gla", "r", m), GR[:, m, :], LAT, ACT.Silu)
            for h in range(GH):
                act.wait_ge(kt_ready, h + 1)
                act.activation(GKT[:, h, :], ps[:, TB:TB + LAT], ACT.Copy).then_inc(kt_free, 1)
            for h in range(GH):
                for c in range(2):
                    act.wait_ge(o_ready, h * NCH + 8 * (c + 1))
                    for half in range(2):
                        b = 4 + 2 * c + half
                        act.activation(HG[:, 2 * h + half, c * 512:(c + 1) * 512], ps[:, b * BANK:(b + 1) * BANK], ACT.Copy)\
                           .then_inc(oe_ready, 1)
            act.wait_ge(oe_ready, 4 * GH)
            for h in range(GH):
                for j in range(2):
                    if j:
                        act.wait_ge(sq_used, SQU_BASE["glaN"] + h + 1)
                    elif h:
                        act.wait_ge(ps_ready, TINDEX[("glaN", "ssq", h - 1)] + 1)
                    act.activation(S01[:, 0, :], HG[:, 2 * h + j, :], ACT.Square).then_inc(sq_ready, 1)
                root("glaN", h, S01[:, 1, :])
            squares("n4")
            root("n4", 0, NRS("n4"))
            for m in range(UP_T):
                t, o = ready("up", "up", m)
                i = up_ffn(m)
                if m >= 4:
                    act.wait_ge(fm_ready, m // 2 - 1)
                act.activation(FACC[:, m % 4, :], ps[:, o:o + LAT], ACT.Identity, bias=vcol("ffn_b", i),
                               scale=vcol("ffn_w", 3 * i + 2)).then_inc(fa_ready, 1)
                if m % 2 == 1:
                    act.wait_ge(fc_ready, m)
                    act.activation(FACC[:, (m - 1) % 4, :], FACC[:, (m - 1) % 4, :], ACT.Silu).then_inc(fs_ready, 1)
            squares("n5")
            root("n5", 0, NRS("n5"))

        @block.vector
        def _(dve):
            count = [0]

            def link(ins):
                count[0] += 1
                ins.then_inc(dve_done, 1)
                dve.wait_ge(dve_done, count[0])

            def ready(ph, kind, i=0):
                t, o = tile(ph, kind, i)
                dve.wait_ge(ps_ready, t + 1)
                return t, o

            def mean_square(name, i, o, t, rs, width, n):
                dve.tensor_scalar(rs, ps[:, o:o + width], 1.0 / n, EPS, ALU.mult, ALU.add).then_inc(ps_free[t % 2], 1)
                dve.wait_ge(ps_free[t % 2], t // 2 + 1)
                dve.engine_nop().then_inc(ms_ready, 1)
                dve.wait_ge(sd_ready, MS_BASE[name] + i + 1)
                link(dve.reciprocal(rs, rs))

            def norm(ph, gain=None, dst=None):
                t, o = ready(ph, "nrm")
                full = ph in NORM_CTX
                rs = NRS(ph)
                mean_square(ph, 0, o, t, rs, TOK if full else LAT, D)
                for k in range(KT):
                    if full:
                        dve.tensor_tensor(H[:, k, LAT:TOK], XCv[:, k, :], rs[:, LAT:TOK], ALU.mult)
                        dve.tensor_tensor(H[:, k, 0:LAT], XL[:, k, :], rs[:, 0:LAT], ALU.mult).then_inc(hn, 1)
                    else:
                        dve.scalar_tensor_tensor(dst(k), XL[:, k, :], vcol(gain, k), rs, ALU.mult, ALU.mult).then_inc(h_ready, 1)
                if full:
                    dve.wait_ge(hn, 8 * int(ph[1]) + 8)
                else:
                    dve.wait_ge(h_ready, 8 * int(ph[1]) + 8)

            def finish_mod(layer, src):
                mb = vcol("mod_b", 24 * layer, 24).unsqueeze(2).to_broadcast([P, 24, 2])
                link(dve.tensor_tensor(MOD[:, layer], src, mb, ALU.add))
                ng = vcol("norm_g", 8 * layer, 8).unsqueeze(2).to_broadcast([P, KT, 2])
                dve.scalar_tensor_tensor(MA[:, layer], MOD[:, layer, 8:16, :], 1.0, ng, ALU.add, ALU.mult).then_inc(mod_ready, 1)

            dve.wait_ge(loads, 64)
            link(dve.tensor_scalar(GQ[:, :], vcol("q_gain"), scale_q, None, ALU.mult))
            t, o = ready("mod0", "mod")
            finish_mod(0, ps[:, o:o + 48].rearrange("p (m a) -> p m a", a=2))
            dve.wait_ge(mod_ready, 1)
            dve.engine_nop().then_inc(ps_free[t % 2], 1)
            norm("n0")

            n_rope = [0]

            def rope(m):
                if n_rope[0]:
                    dve.wait_ge(qk_done, n_rope[0])
                n_rope[0] += 1
                x = QK[:, m, 0:LAT]
                link(dve.stream_shuffle(SW, x, [i ^ 1 for i in range(32)]))
                link(dve.tensor_tensor(x, x, ROPE[:, 0, :], ALU.mult))
                link(dve.tensor_tensor(SW, SW, ROPE[:, 1, :], ALU.mult))
                dve.tensor_tensor(x, x, SW, ALU.add).then_inc(qk_done, 1)

            def even_half(ph, first):
                if first:
                    dve.wait_ge(rope_in, 16)
                def qknorm(m):
                    t, o = ready(ph, "ssq", m)
                    mean_square("evA", m, o, t, RS, TOK, DH)
                    dve.wait_ge(sq_ready, SQ_BASE["evA"] + m + 1)
                    gain = GQ[:, 0:1] if m < 4 else vcol("k_gain")
                    link(dve.scalar_tensor_tensor(QK[:, m, :], QK[:, m, :], gain, RS, ALU.mult, ALU.mult))
                    rope(m)

                for m in range(5):
                    if first:
                        if m >= 1:
                            qknorm(m - 1)
                    else:
                        dve.wait_ge(raw_ready, m + 1)
                        rope(m)
                for i in range(TOK // P):
                    t, o = ready(ph, "v", i)
                    if not first and i == 0:
                        dve.wait_ge(att["A"]["pv"], 80)
                    dve.tensor_copy(VE[:, i, :], ps[:, o:o + P]).then_inc(ps_free[t % 2], 1)
                    dve.wait_ge(ps_free[t % 2], t // 2 + 1)
                    dve.engine_nop().then_inc(v_ready, 1)
                if first:
                    qknorm(4)

            def attention(name):
                at = att[name]
                units = at["units"]
                for st in at["plan"]:
                    if st["NORM"] is not None:
                        g = st["NORM"]
                        s = g % 2
                        dve.wait_ge(at["pv"], (g + 1) * HEADS)
                        dve.wait_ge(at["exped"], (g + 1) * HEADS)
                        if at["sink"]:
                            dve.wait_ge(at["sink_out"], g + 1)
                            link(dve.tensor_tensor(ST[:, s, 2, :], ST[:, s, 2, :], ST[:, s, 3, :], ALU.add))
                        link(dve.reciprocal(ST[:, s, 2, :], ST[:, s, 2, :]))
                        dve.tensor_tensor(at["ON"].rearrange("p (h d) -> p h d", d=DH),
                                          ps[:, OB:OB + 512].rearrange("p (h d) -> p h d", d=DH),
                                          ST[:, s, 2, :].unsqueeze(2).to_broadcast([P, HEADS, DH]), ALU.mult)\
                           .then_inc(at["normed"], 1)
                    for tg, u, j, n, eng in st["T"]:
                        if eng == "dve":
                            dve.wait_ge(at["t_ready"], tg + 1)
                            dve.tensor_copy(at["PT"][:, u % 2, j * P:(j + n) * P], ps[:, tbank(at, tg):tbank(at, tg) + n * P])\
                               .then_inc(tfree(at, tg)[0], 1)
                    if st["OT"]:
                        tg, g = st["OT"]
                        a, b = units[g * HEADS]["gate"]
                        dve.wait_ge(at["t_ready"], tg + 1)
                        gv = at["gate"](a, b)
                        tb = tbank(at, tg)
                        dve.tensor_tensor(gv, ps[:, tb:tb + 512].rearrange("p (m q) -> p m q", m=4), gv, ALU.mult)\
                           .then_inc(tfree(at, tg)[0], 1)
                        dve.wait_ge(*tfree(at, tg))
                        dve.engine_nop().then_inc(at["mixed"], 1)
                    if st["MOD"]:
                        tg, m0 = st["MOD"]
                        dve.wait_ge(at["t_ready"], tg + 1)
                        tb = tbank(at, tg)
                        dve.tensor_copy(MOD[:, 1, m0:m0 + 3, :], ps[:, tb:tb + 6].rearrange("p (m a) -> p m a", a=2))\
                           .then_inc(tfree(at, tg)[0], 1)
                    if st["S"] is not None:
                        u = st["S"]
                        un = units[u]
                        g, h = divmod(u, HEADS)
                        c0, c1 = un["span"]
                        o = (u % 2) * SLOT
                        dve.wait_ge(at["scores"], u + 1)
                        mx, nm = ST[:, g % 2, 0, h:h + 1], ST[:, g % 2, 1, h:h + 1]
                        if un["mask"] is None:
                            if at["sink"]:
                                link(dve.tensor_reduce(mx, ps[:, o + c0:o + c1], AX_X, ALU.max))
                            else:
                                dve.tensor_reduce(nm, ps[:, o + c0:o + c1], AX_X, ALU.max, negate=True).then_inc(at["maxed"], 1)
                        else:
                            pt = at["P"][:, u % 2, 0:c1 - c0]
                            if u >= 2:
                                dve.wait_ge(at["t_ready"], tgs(at, u - 2)[-1][0] + 1)
                            if un["mask"] == "grid":
                                cls = D_CLASS[g]
                                dve.wait_ge(bias_ready, cls * HEADS + h + 1)
                                link(dve.tensor_tensor_reduce(pt[:, 0:D_LOCAL], ps[:, o:o + D_LOCAL],
                                                              BT[:, cls % 2, h * D_LOCAL:(h + 1) * D_LOCAL], 1.0, -3e38,
                                                              ALU.add, ALU.max, mx))
                                link(dve.tensor_tensor_reduce(pt[:, D_LOCAL:D_LOCAL + CTX], ps[:, o + D_LOCAL:o + c1],
                                                              ZERO, 1.0, mx, ALU.add, ALU.max, nm))
                                dve.tensor_scalar(nm, nm, -1.0, None, ALU.mult).then_inc(at["maxed"], 1)
                            else:
                                link(dve.tensor_tensor_reduce(pt, ps[:, o + c0:o + c1], un["mask"], 1.0, -3e38,
                                                              ALU.add, ALU.max, mx))
                        if at["sink"]:
                            dve.scalar_tensor_tensor(nm, mx, -1.0, NSINK[:, h:h + 1], ALU.mult, ALU.min).then_inc(at["maxed"], 1)
                            if h == HEADS - 1:
                                dve.wait_ge(at["maxed"], u + 1)
                                dve.tensor_tensor(ST[:, g % 2, 3, :], ST[:, g % 2, 1, :], vcol("sink", 0, 8), ALU.add)\
                                   .then_inc(at["sink_in"], 1)

            link(dve.tensor_scalar(NSINK[:, :], vcol("sink", 0, 8), -1.0, None, ALU.mult))
            even_half("evA", True)
            attention("A")
            link(dve.tensor_copy(MODRAW[:, :, :], MOD[:, 1]))
            finish_mod(1, MODRAW[:, :, :])
            even_half("evB", False)
            dve.wait_ge(bmask_in, 16)
            attention("B")

            def residual(ph, gated):
                for m in range(KT):
                    t, o = ready(ph, "res", m)
                    if gated is None:
                        dve.tensor_tensor(XL[:, m, :], ps[:, o:o + LAT], XL[:, m, :], ALU.add).then_inc(ps_free[t % 2], 1)
                    else:
                        if gated == 0:
                            dve.scalar_tensor_tensor(XCv[:, m, :], ps[:, o + LAT:o + TOK], MOD[:, 0, 16 + m, 1:2], XCv[:, m, :],
                                                     ALU.mult, ALU.add)
                        dve.scalar_tensor_tensor(XL[:, m, :], ps[:, o:o + LAT], MOD[:, gated, 16 + m, 0:1], XL[:, m, :],
                                                 ALU.mult, ALU.add).then_inc(ps_free[t % 2], 1)
                    dve.wait_ge(ps_free[t % 2], t // 2 + 1)
                    dve.engine_nop().then_inc(x_done, 1)

            residual("evO", 0)
            norm("n1")
            dve.wait_ge(u_zero, 2)
            for j in range(4):
                t, o = ready("od", "cv", j)
                dve.wait_ge(sig_ready, j + 1)
                dve.tensor_tensor(U[:, j, PAD:PAD + LAT], ps[:, o:o + LAT], SG, ALU.mult).then_inc(ps_free[t % 2], 1)
                dve.wait_ge(ps_free[t % 2], t // 2 + 1)
                dve.engine_nop().then_inc(u_done, 1)
            for j in range(4):
                acc = XC[:, (j % 2) * LAT:(j % 2 + 1) * LAT]
                if j >= 2:
                    dve.wait_ge(conv_done, j - 1)
                w = VOFF["conv_w"] + CONV * j
                link(dve.tensor_scalar(acc, U[:, j, 0:LAT], V[:, w:w + 1], vcol("conv_b", j), ALU.mult, ALU.add))
                for k in range(1, CONV):
                    link(dve.scalar_tensor_tensor(acc, U[:, j, k:k + LAT], V[:, w + k:w + k + 1], acc, ALU.mult, ALU.add))
                dve.tensor_copy(U[:, j, PAD:PAD + LAT], acc).then_inc(conv_done, 1)
            t, o = ready("od", "lnm")
            for j in range(4):
                dve.scalar_tensor_tensor(U[:, j, PAD:PAD + LAT], ps[:, o:o + LAT], -1.0 / 512, U[:, j, PAD:PAD + LAT],
                                         ALU.mult, ALU.add).then_inc(ln_sub, 1)
            dve.wait_ge(ln_sub, 4)
            dve.engine_nop().then_inc(ps_free[t % 2], 1)
            t, o = ready("od", "lnv")
            mean_square("ln", 0, o, t, XC[:, LAT:2 * LAT], LAT, 512)
            for j in range(4):
                dve.tensor_tensor(U[:, j, PAD:PAD + LAT], U[:, j, PAD:PAD + LAT], XC[:, LAT:2 * LAT], ALU.mult).then_inc(ln_mul, 1)
            for j in range(4):
                dve.wait_ge(ln_act, j + 1)
                dve.wait_ge(g_ready, G_BASE["cg"] + j + 1)
                dve.tensor_tensor(CG[:, j, :], CG[:, j, :], U[:, j, PAD:PAD + LAT], ALU.mult).then_inc(mix_ready, 1)
            dve.wait_ge(mix_ready, 4)
            dve.wait_ge(g_ready, G_BASE["od_end"])
            link(dve.memset(ZERO, 0.0))
            attention("D")
            residual("odO", 1)
            norm("n2", "final_g", lambda k: XL[:, k, :])
            norm("n3", "mix_g", lambda k: HG[:, k, :])

            dve.wait_ge(pool_done, 2)
            for m in range(4):
                t, o = ready("gla", "z", m)
                if m:
                    dve.wait_ge(kd_ready, m)
                link(dve.tensor_scalar(S01[:, 0, :], ps[:, o:o + LAT], vcol("gate_b", m), None, ALU.add))
                dve.engine_nop().then_inc(ps_free[t % 2], 1)
                dve.engine_nop().then_inc(zb_ready, 1)
                dve.wait_ge(sp_ready, m + 1)
                link(dve.scalar_tensor_tensor(S01[:, 1, :], S01[:, 0, :], 0.0, S01[:, 1, :], ALU.min, ALU.subtract))
                link(dve.tensor_tensor_scan(S01[:, 0, :], SMASK, S01[:, 1, :], 0.0, ALU.mult, ALU.add))
                gs = S01[:, 0, :].rearrange("p (c s) -> p c s", s=CHUNK)
                dve.tensor_tensor(S01[:, 1, :].rearrange("p (c s) -> p c s", s=CHUNK),
                                  gs[:, :, CHUNK - 1:CHUNK].to_broadcast([P, NCH, CHUNK]), gs, ALU.subtract).then_inc(gc_ready, 1)
                dve.wait_ge(ge_ready, m + 1)
                dve.wait_ge(g_ready, G_BASE["od_end"] + m + 1)
                dve.tensor_tensor(GKT[:, m, :], GKT[:, m, :], S01[:, 1, :], ALU.mult).then_inc(kd_ready, 1)
            for i in range(GH * NCH):
                h, c = divmod(i, NCH)
                dve.wait_ge(kv_ready, i + 1)
                if i >= 2:
                    dve.wait_ge(o_ready, i - 1)
                if i:
                    dve.wait_ge(st_ready, i)
                kv = ps[:, (i % 4) * BANK:(i % 4) * BANK + GDV]
                if c == 0:
                    dve.tensor_copy(STATE[:, i % 2, :], kv).then_inc(st_ready, 1)
                else:
                    dve.scalar_tensor_tensor(STATE[:, i % 2, :], STATE[:, (i - 1) % 2, :], DEC[:, h, c:c + 1], kv,
                                             ALU.mult, ALU.add).then_inc(st_ready, 1)
            for h in range(GH):
                t, o = ready("glaN", "ssq", h)
                if h:
                    dve.wait_ge(gm_ready, 2 * h)
                mean_square("glaN", h, o, t, S01[:, 1, :], LAT, GDV)
                for j in range(2):
                    x = HG[:, 2 * h + j, :]
                    link(dve.scalar_tensor_tensor(x, x, vcol("gla_g", 2 * h + j), S01[:, 1, :], ALU.mult, ALU.mult))
                    dve.tensor_tensor(GR[:, 2 * h + j, :], GR[:, 2 * h + j, :], x, ALU.mult).then_inc(gm_ready, 1)
            residual("glaO", None)
            norm("n4", "ffn_g", lambda k: HG[:, k, :])
            for m in range(UP_T):
                t, o = tile("up", "up", m)
                i = up_ffn(m)
                dve.wait_ge(fa_ready, m + 1)
                link(dve.scalar_tensor_tensor(FACC[:, m % 4, 1:LAT], ps[:, o:o + LAT - 1], vcol("ffn_w", 3 * i + 1),
                                              FACC[:, m % 4, 1:LAT], ALU.mult, ALU.add))
                dve.scalar_tensor_tensor(FACC[:, m % 4, 2:LAT], ps[:, o:o + LAT - 2], vcol("ffn_w", 3 * i),
                                         FACC[:, m % 4, 2:LAT], ALU.mult, ALU.add).then_inc(fc_ready, 1)
                dve.wait_ge(fc_ready, m + 1)
                dve.engine_nop().then_inc(ps_free[t % 2], 1)
                if m % 2 == 1:
                    dve.wait_ge(fs_ready, m // 2 + 1)
                    dve.tensor_tensor(ACTV[:, m // 2, :], FACC[:, (m - 1) % 4, :], FACC[:, m % 4, :], ALU.mult).then_inc(fm_ready, 1)
            residual("down", None)
            norm("n5", "out_g", lambda k: XL[:, k, :])


def kernel(**inputs):
    import numpy as np
    import concourse.bacc as bacc
    from concourse.bass_utils import run_bass_kernel_spmd as run

    x = {k: np.asarray(v) for k, v in inputs.items()}

    def tiles(w):
        k, m = w.shape
        return w.reshape(k // P, P, m // P, P).transpose(2, 1, 0, 3).reshape(m // P, P, k)

    def cols(v):
        return v.reshape(-1, P).T

    even = x["ev_w_in"][0]
    parts = {}
    at = 0
    for name, width in (("aq", 512), ("ak", 128), ("av", 128), ("ag", 512), ("bq", 512), ("bk", 128), ("bv", 128), ("bg", 512)):
        parts[name] = even[:, at:at + width]
        at += width
    order = np.concatenate([np.arange(h * DH, (h + 1) * DH) for t in range(4) for h in (t, t + 4)])
    ev = {s: np.concatenate([parts[s + "q"][:, order], parts[s + "k"], parts[s + "v"], parts[s + "g"]], axis=1) for s in "ab"}
    od = tiles(x["od_w_in"][0])
    cv, cgl, cg, dq, dk, dv, dg = (od[4 * i:4 * i + 4] for i in range(7))
    gla = tiles(x["gla_w_in_2"][0][:, :3072])
    up = tiles(x["ffn_w_up_2"][0])
    wall = np.concatenate([
        tiles(x["mod_w"][0]), tiles(ev["a"]), tiles(x["mod_w"][1]), tiles(ev["b"]), tiles(x["ev_w_out"][0]),
        np.stack([t for pair in zip(cgl, cv) for t in pair]), dv, cg, dq, dk, dg, tiles(x["od_w_out"][0]),
        gla[4:8], gla[8:16], gla[0:4], gla[16:24], tiles(x["gla_w_out_2"][0]),
        np.stack([t for pair in zip(up[:DOWN_K], up[DOWN_K:]) for t in pair])])
    wdown = tiles(x["ffn_w_down_2"][0])
    wglr = x["gla_w_in_2"][0][:, 3072:].reshape(KT, P, 16).transpose(1, 0, 2).reshape(P, KT * 16)
    vec = np.concatenate([
        np.stack([cols(x["c"][0]), cols(x["c_ctx"])], axis=2).reshape(P, 16),
        cols(x["mod_b"].reshape(-1)), cols(x["norm_g"].reshape(-1)),
        np.tile(x["a_q_gain"][0], 2)[:, None], np.tile(x["a_k_gain"][0], 2)[:, None],
        np.broadcast_to(x["b_sink"][0][None], (P, 8)),
        x["c_dw_w"][0].reshape(CONV, 4, P).transpose(2, 1, 0).reshape(P, 4 * CONV), cols(x["c_dw_b"][0]),
        cols(x["c_ln_g"][0]), cols(x["c_ln_b"][0]), cols(x["final_g"]), cols(x["mix_norm_w_2"][0]),
        cols(x["ffn_norm_w_2"][0]), cols(x["final_norm_w_2"]), cols(x["gla_b_gate_2"][0]), cols(x["gla_norm_w_2"][0]),
        x["ffn_conv_w_2"][0].reshape(3, UP_T, P).transpose(2, 1, 0).reshape(P, 3 * UP_T), cols(x["ffn_conv_b_2"][0])], axis=1)

    def feature_major(a):
        return a[0].T.reshape(KT, P, -1).transpose(1, 0, 2)

    f = np.float32
    consts = np.concatenate([np.eye(P), np.ones((P, P)), np.kron(np.eye(2), np.ones((64, 64)))], axis=1).astype(f)
    pos = np.arange(LAT)
    freqs = (f(10000.0) ** (-np.arange(0, DH // 2, 2, dtype=f) / f(DH // 2))).astype(f)
    ang = np.concatenate([(pos // GRID).astype(f)[:, None] * freqs, (pos % GRID).astype(f)[:, None] * freqs], axis=1)
    pair = (np.arange(P) % DH) // 2
    sign = np.where(np.arange(P) % 2 == 0, -1.0, 1.0)[:, None]
    ropes = np.stack([np.cos(ang).T[pair], np.sin(ang).T[pair] * sign], axis=1).astype(f)
    p, c = np.arange(P)[:, None], np.arange(384)[None]
    band = np.where((c >= p) & (c <= p + 256), 0.0, -1e30)
    zero = np.zeros((P, CTX))
    bmask = np.concatenate([band, zero, band[:, :256], zero], axis=1).astype(f)
    dmask = np.zeros((5, P, 10, GRID), f)
    cs = np.clip(np.arange(GRID) - 8, 0, GRID - 16)[:, None]
    kc = np.arange(GRID)[None]
    in_cols = (kc >= cs) & (kc < cs + 16)
    for cls in range(5):
        qt = D_CLASS.index(cls)
        for half in range(2):
            rs = min(max(2 * qt + half - 4, 0), 8)
            for i in range(10):
                row_in = rs <= D_BASE[qt] + i < rs + 8
                dmask[cls, 64 * half:64 * half + 64, i] = np.where(in_cols & row_in, 0.0, -1e30)
    dmask = dmask.reshape(5, P, D_LOCAL)
    rpb = np.zeros((8, RPB_ROWS, 31), f)
    rpb[:, 2:17] = x["d_rpb"][0]
    rpb = np.pad(rpb.reshape(1, -1), ((0, 0), (RPB_PAD, RPB_PAD)))

    arrays = {"wall": wall, "wdown": wdown, "wglr": wglr, "wgate2": x["gla_w_gate2_2"][0], "vec": vec,
              "xl_in": feature_major(x["x"]), "xc_in": feature_major(x["ctx"]), "consts": consts, "ropes": ropes,
              "bmask": bmask, "dmask": dmask, "rpb": rpb}
    arrays = {k: np.ascontiguousarray(v) for k, v in arrays.items()}
    nc = bacc.Bacc("TRN2", target_bir_lowering=False, num_devices=1)
    args = {k: nc.dram_tensor(f"in_{k}", v.shape, F32, kind="ExternalInput").ap() for k, v in arrays.items()}
    out = nc.dram_tensor("out", (P, KT, LAT), F32, kind="ExternalOutput").ap()
    program(nc, **args, out=out)
    got = run(nc, [{f"in_{k}": v for k, v in arrays.items()}], core_ids=[0]).results[0]["out"]
    return got.transpose(1, 0, 2).reshape(D, LAT).T[None]
```

```python
from contextlib import ExitStack

import concourse.bass as bass
from concourse import mybir
from concourse.alu_op_type import AluOpType as ALU

ACT = mybir.ActivationFunctionType
F32 = mybir.dt.float32
AX_X = mybir.AxisListType.X

P = 128
LAT, CTX, D = 1024, 256, 1024
TOK = LAT + CTX
KT = D // P
BANK = 512
SLOT = 3 * BANK
HEADS, DH, QT = 8, 64, LAT // P
EPS = 1e-6
WSLOTS = 4
UP_T, DOWN_K = 44, 22
GH, GDV, CHUNK, NCH = 4, 256, 64, LAT // 64
CONV = 31
PAD = CONV // 2
GRID = 64
D_LOCAL = 10 * GRID
D_BASE = [min(max(2 * j - 4, 0), 6) for j in range(QT)]
D_CLASS = [0, 1, 2, 2, 2, 2, 3, 4]

MOD0 = 16
STREAM = [("mod0", MOD0), ("evA", 10), ("evB", 10 + 8), ("evO", 8 + 24), ("od", 28), ("odO", 8),
          ("gla", 24), ("glaO", 8), ("up", UP_T)]
GBASE, NW = {}, 0
for _n, _c in STREAM:
    GBASE[_n] = NW
    NW += _c

VEC = [("c", 16), ("mod_b", 48), ("norm_g", 16), ("q_gain", 1), ("k_gain", 1), ("sink", 8), ("conv_w", 4 * CONV),
       ("conv_b", 4), ("ln_g", 4), ("ln_b", 4), ("final_g", 8), ("mix_g", 8), ("ffn_g", 8), ("out_g", 8),
       ("gate_b", 4), ("gla_g", 8), ("ffn_w", 3 * UP_T), ("ffn_b", UP_T)]
VOFF, NV = {}, 0
for _n, _c in VEC:
    VOFF[_n] = NV
    NV += _c


RPB_ROWS, RPB_PAD = 20, 64


def RPB_AT(h, e):
    return RPB_PAD + (h * RPB_ROWS + e) * 31 + 15


def product_tiles():
    out = [("n0", "nrm", 0), ("mod0", "mod", 0)]
    for ph in ("evA", "evB"):
        for m in range(5):
            out.append((ph, "qk", m))
            if ph == "evA" and m >= 1:
                out.append((ph, "ssq", m - 1))
        out += [(ph, "v", i) for i in range(TOK // P)]
        if ph == "evA":
            out.append((ph, "ssq", 4))
        out += [(ph, "gate", m) for m in range(4)]
    out += [("evO", "res", m) for m in range(KT)]
    out += [("n1", "nrm", 0)]
    for j in range(4):
        out += [("od", "cgl", j), ("od", "cv", j)]
    out += [("od", "v", i) for i in range(TOK // P)]
    out += [("od", "cg", j) for j in range(4)]
    out += [("od", "dq", j) for j in range(4)]
    out += [("od", "lnm", 0), ("od", "dk", 0), ("od", "dk", 1), ("od", "lnv", 0), ("od", "dk", 2), ("od", "dk", 3)]
    out += [("od", "dg", j) for j in range(4)]
    out += [("odO", "res", m) for m in range(KT)]
    out += [("n2", "nrm", 0), ("n3", "nrm", 0)]
    out += [("gla", "k", m) for m in range(4)] + [("gla", "glr", 0)]
    for m in range(4):
        out += [("gla", "z", m)] + [("gla", "v", 4 * m + i) for i in range(4)]
    out += [("gla", "q", m) for m in range(4)]
    out += [("gla", "r", m) for m in range(8)]
    out += [("glaN", "ssq", h) for h in range(GH)]
    out += [("glaO", "res", m) for m in range(KT)]
    out += [("n4", "nrm", 0)]
    out += [("up", "up", m) for m in range(UP_T)]
    out += [("down", "res", m) for m in range(KT)]
    out += [("n5", "nrm", 0)]
    return out


TILES = product_tiles()
TINDEX = {key: t for t, key in enumerate(TILES)}


def attention_plan(units, heads_per_group):
    n = len(units)
    groups = n // heads_per_group
    steps, tg = [], 0
    for s in range(n + 6):
        st = {"S": s if s < n else None, "T": [], "PV": s - 3 if 0 <= s - 3 < n else None,
              "NORM": None, "OT": None, "X": s - 1 if 0 <= s - 1 < n else None}
        u = s - 2
        if 0 <= u < n:
            nt = units[u]["nt"]
            for i, j in enumerate(range(0, nt, 4)):
                st["T"].append((tg, u, j, min(4, nt - j), "act" if i else "dve"))
                tg += 1
        v = s - 4
        if 0 <= v < n and v % heads_per_group == heads_per_group - 1:
            st["NORM"] = v // heads_per_group
            st["OT"] = (tg, v // heads_per_group)
            tg += 1
        steps.append(st)
    assert groups * heads_per_group == n
    return steps


def program(nc, wall, wdown, wglr, wgate2, vec, xl_in, xc_in, consts, ropes, bmask, dmask, rpb, out):
    with ExitStack() as ctx:
        def sb(name, shape):
            return ctx.enter_context(nc.sbuf_tensor(name, shape, F32))

        def sem(name):
            return ctx.enter_context(nc.semaphore(name))

        XL = sb("x_lat", [P, KT, LAT])
        XC = sb("x_ctx", [P, KT * CTX])
        XCv = XC[:, :].rearrange("p (k n) -> p k n", k=KT)
        CST = sb("consts", [P, 3 * P])
        IDENT, ONES, BONES = CST[:, 0:P], CST[:, P:2 * P], CST[:, 2 * P:3 * P]
        V = sb("vectors", [P, NV])
        SC = sb("silu_c", [P, KT, 2])
        MOD = sb("modulation", [P, 2, 24, 2])
        MA = sb("mod_scale", [P, 2, KT, 2])
        GQ = sb("q_gain_scaled", [P, 1])
        ST = sb("softmax_stats", [P, 2, 4, 8])
        DEC = sb("chunk_decay", [P, GH, NCH])
        NSINK = sb("negated_sink", [P, HEADS])
        MODRAW = sb("modulation_raw", [P, 24, 2])
        ARENA = 41760
        A = sb("arena", [P, ARENA])
        expanded = nc.dram_tensor("expanded_bias", (HEADS, RPB_ROWS, GRID, GRID), F32, kind="Internal").ap()
        ps = ctx.enter_context(nc.psum_tensor("ps", [P, 8 * BANK], F32))

        def area(off, *shape):
            n = 1
            for x in shape:
                n *= x
            assert off + n <= ARENA, (off, n)
            v = A[:, off:off + n]
            if len(shape) == 2:
                v = v.rearrange("p (a b) -> p a b", a=shape[0])
            return v

        def vcol(name, i=0, n=1):
            return V[:, VOFF[name] + i:VOFF[name] + i + n]

        W = area(0, WSLOTS, KT * P).rearrange("p s (k m) -> p s k m", k=KT)
        H = area(4096, KT, TOK)
        QK = area(14336, 5, TOK)
        VE = area(20736, TOK // P, P)
        G = area(22016, KT, TOK)
        ROPE = area(32256, 2, LAT)
        SCR = 34304
        SQ = area(SCR, 2, TOK)
        RS = area(SCR + 2 * TOK, TOK)
        SW = area(SCR + 3 * TOK, LAT)
        U = area(14336, 4, LAT + 2 * PAD)
        CG = area(18552, 4, LAT)
        DQ = area(22648, 4, LAT)
        DK = area(26744, 4, TOK)
        DV = area(31864, TOK // P, 512)
        DG = area(36984, 4, LAT)
        BT = area(4096, 2, HEADS * D_LOCAL)
        HG = area(4096, KT, LAT)
        GQT = area(12288, 4, LAT)
        GKT = area(16384, 4, LAT)
        GV = area(20480, QT, D)
        GR = area(28672, KT, LAT)
        GLR = area(36864, LAT)
        SMASK = area(37888, LAT)
        S01 = area(38912, 2, LAT)
        STATE = area(40960, 2, GDV)
        ACTV = area(12288, DOWN_K, LAT)
        FACC = area(34816, 4, LAT)
        WD = [area(38912, DOWN_K, P), area(0, DOWN_K, P)]
        SG = area(36984, LAT)
        ZERO = area(41080, CTX)
        GSMALL_2 = XC[0:16, 0:512]
        GSMALL_W = XC[:, 512:512 + KT * 16]
        GSMALL_Wv = GSMALL_W.rearrange("p (k m) -> p k m", k=KT)

        def NSQ(ph, k):
            return {"n0": SQ, "n1": SQ, "n2": area(14336, 2, LAT), "n3": area(14336, 2, LAT),
                    "n4": area(12288, 2, LAT), "n5": area(4096, 2, LAT)}[ph][:, k % 2, :]

        def NRS(ph):
            return {"n0": RS, "n1": RS, "n2": area(16384, LAT), "n3": area(17408, LAT), "n4": area(14336, LAT),
                    "n5": area(6144, LAT)}[ph]

        def up_ffn(m):
            return m // 2 + (m % 2) * DOWN_K

        w_in = [sem(f"weights_in_slot{i}") for i in range(WSLOTS)]
        w_mod = sem("mod_weights_used")
        ps_ready = sem("product_ready")
        ps_free = [sem(f"product_slot{i}_free") for i in range(2)]
        dve_done = sem("dve_step")
        act_done = sem("act_step")
        pool_done = sem("pool_step")
        first_loads = sem("vectors_and_constants_in")
        x_in = [sem(f"residual_pair{i}_in") for i in range(KT // 2)]
        rope_in = sem("rope_in")
        table_in = sem("bias_table_expanded")
        small_in = sem("gla_small_in")
        bmask_in = sem("band_mask_in")
        dmask_in = [sem(f"grid_mask_in{i}") for i in range(2)]
        bias_in = [[sem(f"bias_rows_in{i}_heads{2 * q}_{2 * q + 1}") for q in range(4)] for i in range(2)]
        bias_ready = sem("bias_ready")
        down_in = [sem(f"down_weights_in{i}") for i in range(2)]
        silu_c = sem("silu_c_ready")
        mod_ready = sem("modulation_ready")
        late_mod_read = sem("late_modulation_sums_read")
        rows_in_sbuf = sem("modulation_rows_in_sbuf")
        keys_ready = sem("keys_of_each_half_ready")
        q_padded = sem("queries_padded")
        pads_zeroed = sem("query_pads_zeroed")
        x_done = sem("residual_written")
        sq_ready = sem("squares_ready")
        sq_used = sem("squares_summed")
        ms_ready = sem("mean_square_ready")
        sd_ready = sem("root_ready")
        hn = sem("normed_ready")
        h_ready = sem("h_ready")
        qk_done = sem("qk_ready")
        g_ready = sem("act_tiles_ready")
        v_ready = sem("v_ready")
        outs = sem("outputs_written")
        raw_ready = sem("raw_evacuated")
        u_zero = sem("pads_zeroed")
        sig_ready = sem("sigmoid_ready")
        u_done = sem("conv_inputs_ready")
        conv_done = sem("conv_ready")
        ln_sub = sem("centred_ready")
        ln_mul = sem("ln_scaled")
        ln_act = sem("ln_silu_ready")
        mix_ready = sem("conv_mix_ready")
        glr_ready = sem("glr_ready")
        zb_ready = sem("z_ready")
        sp_ready = sem("softplus_ready")
        gc_ready = sem("gate_sums_ready")
        ge_ready = sem("gate_exps_ready")
        kd_ready = sem("decayed_k_ready")
        kt_ready = sem("k_transposed")
        kt_free = sem("k_t_evacuated")
        kv_ready = sem("chunk_kv_ready")
        st_ready = sem("state_ready")
        o_ready = sem("chunk_out_ready")
        oe_ready = sem("gla_out_evacuated")
        gm_ready = sem("gla_mix_ready")
        fa_ready = sem("ffn_conv_started")
        fc_ready = sem("ffn_conv_ready")
        fs_ready = sem("ffn_silu_ready")
        fm_ready = sem("ffn_product_ready")

        def slot(t):
            return (t % 2) * SLOT

        def tile(ph, kind, i=0):
            t = TINDEX[(ph, kind, i)]
            return t, slot(t)

        NORM_CTX = ("n0", "n1")
        X_BASE = {"n1": 0, "n2": 8, "n4": 16, "n5": 24}
        G_BASE = {"cg": 10, "od_end": 26, "gla_end": 58}
        H_READY_OUT = 40
        SQU_BASE, b = {}, 0
        for name, n in [("n0", 7), ("n1", 7), ("ln", 3), ("n2", 7), ("n3", 7), ("glaN", 4), ("n4", 7), ("n5", 7)]:
            SQU_BASE[name] = b
            b += n
        SQ_BASE, HN_BASE, H_BASE = {}, {}, {}
        sq_order = [("n0", 8), ("evA", 5), ("n1", 8), ("ln", 4), ("n2", 8), ("n3", 8), ("glaN", 8), ("n4", 8), ("n5", 8)]
        b = 0
        for name, n in sq_order:
            SQ_BASE[name] = b
            b += n
        ms_order = [("n0", 1), ("evA", 5), ("n1", 1), ("ln", 1), ("n2", 1), ("n3", 1), ("glaN", 4), ("n4", 1), ("n5", 1)]
        MS_BASE, b = {}, 0
        for name, n in ms_order:
            MS_BASE[name] = b
            b += n

        scale_q = DH ** -0.5
        KZ = [QK[:, 4, :], area(39936, TOK)]
        def unit_a(qt, h, ctx_q):
            kz = KZ[h // 4]
            qcol = (LAT if ctx_q else 0) + qt * P
            u = {"h": h, "q": QK[:, h % 4, qcol:qcol + P]}
            vs = slice(64 * (h // 4), 64 * (h // 4) + 64)
            if ctx_q:
                u["chunks"] = [(0, kz[:, LAT:TOK], CTX)]
                u["v"] = [VE[:, QT + i, vs] for i in range(2)]
                u["span"] = (0, CTX)
            else:
                u["chunks"] = [(c, kz[:, c:c + n], n) for c, n in ((0, 512), (512, 512), (LAT, CTX))]
                u["v"] = [VE[:, i, vs] for i in range(TOK // P)]
                u["span"] = (0, TOK)
            u["mask"] = None
            u["nt"] = len(u["v"])
            u["gate"] = (qcol, qcol + P)
            return u

        BM = area(SCR + 4 * 640 + BANK, 1152)

        def unit_b(qt, h, ctx_q):
            u = unit_a(qt, h, ctx_q)
            if not ctx_q:
                kz = KZ[h // 4]
                vs = slice(64 * (h // 4), 64 * (h // 4) + 64)
                lo, hi = max(qt - 1, 0), min(qt + 2, QT)
                w = (hi - lo) * P
                u["chunks"] = [(BANK - w, kz[:, lo * P:hi * P], w),
                               (BANK, kz[:, LAT:TOK], CTX)]
                u["span"] = (BANK - w, BANK + CTX)
                u["v"] = [VE[:, i, vs] for i in list(range(lo, hi)) + [QT, QT + 1]]
                u["nt"] = len(u["v"])
                u["mask"] = BM[:, 640:1152] if qt == QT - 1 else BM[:, (128 if qt == 0 else 0):640]
            return u

        QP_N = 4
        QP = XC[:, 2 * D_LOCAL:2 * D_LOCAL + QP_N * P].rearrange("p (s q) -> p s q", s=QP_N)

        def unit_d(qt, h):
            b0 = D_BASE[qt] * GRID
            half = slice(64 * (h % 2), 64 * (h % 2) + 64)
            u = {"h": h, "q": QP[:, h % QP_N, :]}
            u["pad"] = (QP[half, h % QP_N, :], DQ[half, h // 2, qt * P:(qt + 1) * P])
            u["chunks"] = [(0, DK[:, h // 2, b0:b0 + 512], 512), (512, DK[:, h // 2, b0 + 512:b0 + 640], 128),
                           (640, DK[:, h // 2, LAT:TOK], CTX)]
            u["span"] = (0, D_LOCAL + CTX)
            u["v"] = [DV[:, i, h * 64:(h + 1) * 64] for i in list(range(b0 // P, b0 // P + 5)) + [QT, QT + 1]]
            u["nt"] = 7
            u["mask"] = "grid"
            u["gate"] = (qt * P, (qt + 1) * P)
            return u

        att_units = {
            "A": [unit_a(q, h, False) for q in range(QT) for h in range(HEADS)]
            + [unit_a(q, h, True) for q in range(2) for h in range(HEADS)],
            "B": [unit_b(q, h, False) for q in range(QT) for h in range(HEADS)]
            + [unit_b(q, h, True) for q in range(2) for h in range(HEADS)],
            "D": [unit_d(q, h) for q in range(QT) for h in range(HEADS)],
        }
        att = {}
        for name, units in att_units.items():
            width = {"A": TOK, "B": 640, "D": D_LOCAL + CTX}[name]
            base = SCR if name != "D" else 14336
            at = {"units": units, "plan": attention_plan(units, HEADS),
                  "P": area(base, 2, width), "PT": area(base + 2 * width, 2, width),
                  "ON": area(base + 4 * width, BANK),
                  "gate": (lambda a, b: G[:, 0:4, a:b]) if name == "A" else
                          (lambda a, b: G[:, 4:8, a:b]) if name == "B" else
                          (lambda a, b: DG[:, :, a:b]),
                  "sink": name == "B"}
            at["tb"] = [6 * BANK] if name == "A" else [6 * BANK, 2 * BANK]
            at["t_free"] = [sem(f"att{name}_t_free{i}") for i in range(len(at["tb"]))]
            for s in ("scores", "maxed", "exped", "t_ready", "pv", "normed", "sink_in", "sink_out", "mixed"):
                at[s] = sem(f"att{name}_{s}")
            att[name] = at
        TB, OB = 6 * BANK, 7 * BANK
        MROW = area(14336, MOD0 * P)[0:2, :]

        def mod_rows(m, n=1):
            q, r = divmod(m, 4)
            b = (TB if q == 3 else tile("mod0", "mod")[1] + q * BANK) + r * P
            return ps[0:2, b:b + n * P]

        def tbank(at, tg):
            return at["tb"][tg % len(at["tb"])]

        def tfree(at, tg):
            nb = len(at["tb"])
            return at["t_free"][tg % nb], tg // nb + 1

        def tgs(at, u):
            return [x for st in at["plan"] for x in st["T"] if x[1] == u]

        def weights_done(g):
            ph = next(n for n, c in STREAM if GBASE[n] <= g < GBASE[n] + c)
            i = g - GBASE[ph]
            if ph == "mod0":
                return w_mod, i + 1
            if ph == "evO":
                return (ps_ready, TINDEX[(ph, "res", i // 4)] + 1) if i % 4 == 0 else (w_mod, MOD0 + 8 + i - i // 4)
            if ph == "evB" and i >= 6:
                m, r = divmod(i - 6, 3)
                return (ps_ready, TINDEX[(ph, "gate", m)] + 1) if r == 0 else (w_mod, MOD0 + 2 * m + r)
            if ph in ("evA", "evB"):
                key = (ph, "qk", i) if i < 5 else (ph, "v", TOK // P - 1) if i == 5 else (ph, "gate", i - 6)
            elif ph == "od":
                key = ((ph, "cgl" if i % 2 == 0 else "cv", i // 2) if i < 8 else (ph, "v", TOK // P - 1) if i < 12 else
                       (ph, ("cg", "dq", "dk", "dg")[(i - 12) // 4], i % 4))
            elif ph == "gla":
                key = ((ph, "k", i) if i < 4 else (ph, "v", QT - 1) if i < 8 else (ph, "v", 2 * QT - 1) if i < 12 else
                       (ph, "q", i - 12) if i < 16 else (ph, "r", i - 16))
            elif ph == "up":
                key = (ph, "up", i)
            else:
                key = (ph, "res", i)
            return ps_ready, TINDEX[key] + 1

        block = ctx.enter_context(nc.Block())

        @block.sync
        def _(sp):
            for dst, src in ((V[:, :], vec), (CST[:, :], consts)):
                sp.dma_start(dst, src).then_inc(first_loads, 16)

            def load_weight(g):
                if g >= WSLOTS:
                    s, v = weights_done(g - WSLOTS)
                    sp.wait_ge(s, v)
                sp.dma_start(A[:, (g % WSLOTS) * 1024:(g % WSLOTS + 1) * 1024], wall[g]).then_inc(w_in[g % WSLOTS], 16)

            for k in range(0, KT, 2):
                sp.dma_start(XL[:, k:k + 2, :], xl_in[:, k:k + 2, :]).then_inc(x_in[k // 2], 16)
                sp.dma_start(XCv[:, k:k + 2, :], xc_in[:, k:k + 2, :]).then_inc(x_in[k // 2], 16)
            for g in range(NW):
                if g == MOD0:
                    sp.dma_start(ROPE, ropes).then_inc(rope_in, 16)
                if g == GBASE["evO"]:
                    sp.wait_ge(qk_done, 10)
                    sp.dma_start(BM, bmask).then_inc(bmask_in, 16)
                load_weight(g)
            for m in range(KT):
                if m == 0:
                    sp.wait_ge(gm_ready, 8)
                    sp.wait_ge(ps_ready, TINDEX[("glaO", "res", 0)] + 1)
                if m == 1:
                    sp.wait_ge(ps_ready, TINDEX[("up", "up", UP_T - 1)] + 1)
                if m >= 2:
                    sp.wait_ge(ps_ready, TINDEX[("down", "res", m - 2)] + 1)
                sp.dma_start(WD[m % 2], wdown[m].rearrange("p (k m) -> p k m", k=DOWN_K)).then_inc(down_in[m % 2], 16)
            for k in range(KT):
                sp.wait_ge(h_ready, H_READY_OUT + k + 1)
                sp.dma_start(out[:, k, :], XL[:, k, :]).then_inc(outs, 16)
            sp.wait_ge(outs, 16 * KT)

        @block.gpsimd
        def _(pool):
            pool.wait_ge(w_mod, MOD0)
            src = bass.AP(rpb.tensor, RPB_AT(0, 0), [[31, HEADS * RPB_ROWS], [-1, GRID], [1, GRID]])
            pool.dma_start(expanded.rearrange("h r q k -> (h r) q k"), src).then_inc(table_in, 16)
            pool.memset(KZ[1][0:64, :], 0.0).then_inc(pool_done, 1)
            for n in range(2):
                pool.wait_ge(qk_done, 5 * (n + 1))
                pool.tensor_copy(KZ[1][64:128, :], KZ[0][64:128, :]).then_inc(pool_done, 1)
                pool.wait_ge(pool_done, 2 * n + 2)
                pool.memset(KZ[0][64:128, :], 0.0).then_inc(pool_done, 1)
                pool.wait_ge(pool_done, 2 * n + 3)
                pool.nop().then_inc(keys_ready, 1)
            pool.wait_ge(att["B"]["mixed"], 10)
            pool.memset(U[:, :, 0:PAD], 0.0).then_inc(u_zero, 1)
            pool.memset(U[:, :, PAD + LAT:LAT + 2 * PAD], 0.0).then_inc(u_zero, 1)

            def bias(cls):
                s = cls % 2
                qt = D_CLASS.index(cls)
                if cls >= 2:
                    last = max(i for i in range(QT) if D_CLASS[i] == cls - 2)
                    pool.wait_ge(att["D"]["maxed"], (last + 1) * HEADS)
                masks = XC[:, s * D_LOCAL:(s + 1) * D_LOCAL]
                pool.dma_start(masks, dmask[cls]).then_inc(dmask_in[s], 16)
                if cls == 0:
                    pool.wait_ge(table_in, 16)
                    pool.wait_ge(ps_ready, TINDEX[("od", "dg", 3)] + 1)

                def rows(q):
                    for h in (2 * q, 2 * q + 1):
                        for half in range(2):
                            e = D_BASE[qt] - 2 * qt - half + 7 + 2
                            dst = BT[64 * half:64 * half + 64, s, h * D_LOCAL:(h + 1) * D_LOCAL].rearrange("p (r c) -> p r c", r=10)
                            src = expanded[h, e:e + 10].rearrange("r q k -> q r k")
                            pool.dma_start(dst, src).then_inc(bias_in[s][q], 16)

                rows(0)
                pool.wait_ge(dmask_in[s], 16 * (cls // 2 + 1))
                for q in range(4):
                    if q < 3:
                        rows(q + 1)
                    pool.wait_ge(bias_in[s][q], 16 * 4 * (cls // 2 + 1))
                    for h in (2 * q, 2 * q + 1):
                        dst = BT[:, s, h * D_LOCAL:(h + 1) * D_LOCAL]
                        pool.tensor_tensor(dst, dst, masks, ALU.add).then_inc(bias_ready, 1)

            pool.wait_ge(mix_ready, 4)
            pool.memset(QP[64:128, 0::2, :], 0.0).then_inc(pads_zeroed, 1)
            pool.memset(QP[0:64, 1::2, :], 0.0).then_inc(pads_zeroed, 1)
            pool.wait_ge(pads_zeroed, 2)
            for cls in range(5):
                bias(cls)
            pool.wait_ge(ps_ready, TINDEX[("odO", "res", KT - 1)] + 1)
            pool.memset(SMASK, 1.0).then_inc(pool_done, 1)
            pool.wait_ge(pool_done, 6)
            pool.memset(SMASK.rearrange("p (c s) -> p c s", s=CHUNK)[:, :, 0:1], 0.0).then_inc(pool_done, 1)
            pool.wait_ge(bias_ready, 5 * HEADS)
            pool.dma_start(GSMALL_W, wglr).then_inc(small_in, 16)
            pool.dma_start(GSMALL_2, wgate2).then_inc(small_in, 16)

        @block.tensor
        def _(pe):
            def wait_slot(t):
                if t >= 2:
                    pe.wait_ge(ps_free[t % 2], t // 2)

            def wait_weight(g):
                pe.wait_ge(w_in[g % WSLOTS], 16 * (g // WSLOTS + 1))

            def product(key, g, rhs, chunks, k_ready=None):
                t, o = tile(*key)
                wait_weight(g)
                wait_slot(t)
                for k in range(KT):
                    if k_ready:
                        pe.wait_ge(*k_ready(k))
                    for c, n in chunks:
                        mm = pe.matmul(ps[:, o + c:o + c + n], W[:, g % WSLOTS, k, :], rhs(k, c, n),
                                       start=(k == 0), stop=(k == KT - 1))
                mm.then_inc(ps_ready, 1)

            full = ((0, 512), (512, 512), (LAT, CTX))
            lat = ((0, 512), (512, 512))

            def hrow(k, c, n):
                return H[:, k, c:c + n]

            def norm_sums(ph):
                t, o = tile(ph, "nrm")
                wait_slot(t)
                pe.wait_ge(sq_used, SQU_BASE[ph] + KT - 1)
                for c, n in (full if ph in NORM_CTX else lat):
                    mm = pe.matmul(ps[:, o + c:o + c + n], ONES, NRS(ph)[:, c:c + n], start=True, stop=True)
                mm.then_inc(ps_ready, 1)

            def group_sums(ph, i, mat, parts, chunks, o, sqs):
                for j in range(parts):
                    for c, n in chunks:
                        mm = pe.matmul(ps[:, o + c:o + c + n], mat, sqs(j)[:, c:c + n], start=(j == 0), stop=(j == parts - 1))
                return mm

            pe.wait_ge(first_loads, 32)
            pe.wait_ge(silu_c, 1)
            t, o = tile("mod0", "mod")
            for m in range(MOD0):
                if m == MOD0 // 2:
                    norm_sums("n0")
                wait_weight(m)
                for k in range(KT):
                    mm = pe.matmul(mod_rows(m), SC[:, k, :], W[:, m % WSLOTS, k, :], start=(k == 0), stop=(k == KT - 1))
                mm.then_inc(w_mod, 1)
            for m in range(MOD0):
                if m % 4 == 0:
                    pe.wait_ge(rows_in_sbuf, m // 4 + 1)
                mm = pe.transpose(ps[:, OB + 2 * m:OB + 2 * m + 2], MROW[:, m * P:(m + 1) * P], IDENT[0:2, 0:2])
            mm.then_inc(ps_ready, 1)

            n_late = [0]

            def late_modulation(gs):
                if n_late[0]:
                    pe.wait_ge(late_mod_read, n_late[0])
                n_late[0] += 1
                for i, g in enumerate(gs):
                    wait_weight(g)
                    for k in range(KT):
                        mm = pe.matmul(ps[:, TB + 2 * i:TB + 2 * i + 2], W[:, g % WSLOTS, k, :], SC[:, k, :],
                                       start=(k == 0), stop=(k == KT - 1))
                    mm.then_inc(w_mod, 1)

            def even_half(ph, first):
                g0 = GBASE[ph]
                def ssq(m):
                    t, o = tile(ph, "ssq", m)
                    wait_slot(t)
                    pe.wait_ge(sq_ready, SQ_BASE["evA"] + m + 1)
                    for c, n in full:
                        mm = pe.matmul(ps[:, o + c:o + c + n], BONES, SQ[:, m % 2, c:c + n], start=True, stop=True)
                    mm.then_inc(ps_ready, 1)

                for m in range(5):
                    product((ph, "qk", m), g0 + m, hrow, full, (lambda k: (h_ready, k + 1)) if first and m == 0 else None)
                    if first and m >= 1:
                        ssq(m - 1)
                wait_weight(g0 + 5)
                for i in range(TOK // P):
                    t, o = tile(ph, "v", i)
                    wait_slot(t)
                    for k in range(KT):
                        mm = pe.matmul(ps[:, o:o + P], H[:, k, i * P:(i + 1) * P], W[:, (g0 + 5) % WSLOTS, k, :],
                                       start=(k == 0), stop=(k == KT - 1))
                    mm.then_inc(ps_ready, 1)
                if first:
                    ssq(4)
                for m in range(4):
                    g = g0 + 6 + (m if first else 3 * m)
                    product((ph, "gate", m), g, hrow, full)
                    if not first:
                        late_modulation((g + 1, g + 2))

            def attention(name, t_next):
                at = att[name]
                units = at["units"]
                for s in range(2):
                    pe.wait_ge(ps_free[s], (t_next + 1 - s) // 2)
                for st in at["plan"]:
                    def scores(i):
                        u = units[st["S"]]
                        c, k, n = u["chunks"][i]
                        o = (st["S"] % 2) * SLOT
                        if i == 0 and name == "D":
                            pe.wait_ge(q_padded, st["S"] + 1)
                        if i == 0 and st["S"] >= 2:
                            pe.wait_ge(at["exped"], st["S"] - 1)
                        mm = pe.matmul(ps[:, o + c:o + c + n], u["q"], k, start=True, stop=True)
                        if i == len(u["chunks"]) - 1:
                            mm.then_inc(at["scores"], 1)

                    def wait_bank(tg):
                        if tg >= len(at["tb"]):
                            pe.wait_ge(*tfree(at, tg - len(at["tb"])))
                        return tbank(at, tg)

                    def transposes(i):
                        tg, u, j, n, _ = st["T"][i]
                        if i == 0:
                            pe.wait_ge(at["exped"], u + 1)
                        tb = wait_bank(tg)
                        for x in range(n):
                            mm = pe.transpose(ps[:, tb + x * P:tb + (x + 1) * P],
                                              at["P"][:, u % 2, (j + x) * P:(j + x + 1) * P], IDENT)
                        mm.then_inc(at["t_ready"], 1)

                    def values(j0, j1):
                        v = st["PV"]
                        u = units[v]
                        if j0 == 0:
                            for x in tgs(at, v):
                                pe.wait_ge(*tfree(at, x[0]))
                            if v % HEADS == 0 and v:
                                pe.wait_ge(at["normed"], v // HEADS)
                        for j in range(j0, j1):
                            mm = pe.matmul(ps[:, OB + u["h"] * 64:OB + u["h"] * 64 + 64],
                                           at["PT"][:, v % 2, j * P:(j + 1) * P], u["v"][j], start=(j == 0), stop=(j == u["nt"] - 1))
                        if j1 == u["nt"]:
                            mm.then_inc(at["pv"], 1)

                    ns = len(units[st["S"]]["chunks"]) if st["S"] is not None else 0
                    nt = units[st["PV"]]["nt"] if st["PV"] is not None else 0
                    for i in range(max(ns, 2)):
                        if i < ns:
                            scores(i)
                        if i < min(len(st["T"]), 2):
                            transposes(i)
                    if nt:
                        values(0, nt // 2)
                    if len(st["T"]) > 2:
                        transposes(2)
                    if st["OT"]:
                        tg, g = st["OT"]
                        pe.wait_ge(at["normed"], g + 1)
                        tb = wait_bank(tg)
                        for x in range(4):
                            mm = pe.transpose(ps[:, tb + x * P:tb + (x + 1) * P], at["ON"][:, x * P:(x + 1) * P], IDENT)
                        mm.then_inc(at["t_ready"], 1)
                    if nt:
                        values(nt // 2, nt)

            even_half("evA", True)
            pe.wait_ge(qk_done, 5)
            pe.wait_ge(keys_ready, 1)
            pe.wait_ge(v_ready, 10)
            attention("A", TINDEX[("evB", "qk", 0)])
            pe.wait_ge(att["A"]["exped"], len(att["A"]["units"]))
            pe.wait_ge(att["A"]["mixed"], 10)
            even_half("evB", False)
            pe.wait_ge(qk_done, 10)
            pe.wait_ge(keys_ready, 2)
            pe.wait_ge(v_ready, 20)
            attention("B", TINDEX[("evO", "res", 0)])
            pe.wait_ge(att["B"]["mixed"], 10)
            for m in range(KT):
                product(("evO", "res", m), GBASE["evO"] + 4 * m, lambda k, c, n: G[:, k, c:c + n], full)
                late_modulation([GBASE["evO"] + 4 * m + 1 + i for i in range(3)])
            norm_sums("n1")

            g0 = GBASE["od"]
            for j in range(4):
                for x, kind in enumerate(("cgl", "cv")):
                    first = j == 0 and x == 0
                    product(("od", kind, j), g0 + 2 * j + x, hrow, lat, (lambda k: (h_ready, 8 + k + 1)) if first else None)
            for i in range(4):
                wait_weight(g0 + 8 + i)
            for i in range(TOK // P):
                t, o = tile("od", "v", i)
                wait_slot(t)
                for k in range(KT):
                    mm = pe.matmul(ps[:, o:o + 512], H[:, k, i * P:(i + 1) * P], W[:, :, k, :],
                                   start=(k == 0), stop=(k == KT - 1))
                mm.then_inc(ps_ready, 1)
            def layer_norm_sums():
                t, o = tile("od", "lnm")
                wait_slot(t)
                for j in range(4):
                    pe.wait_ge(conv_done, j + 1)
                    for c, n in lat:
                        mm = pe.matmul(ps[:, o + c:o + c + n], ONES, U[:, j, PAD + c:PAD + c + n], start=(j == 0), stop=(j == 3))
                mm.then_inc(ps_ready, 1)

            def layer_norm_squares():
                t, o = tile("od", "lnv")
                wait_slot(t)
                for j in range(4):
                    pe.wait_ge(sq_ready, SQ_BASE["ln"] + j + 1)
                    for c, n in lat:
                        mm = pe.matmul(ps[:, o + c:o + c + n], ONES, XC[:, c:c + n], start=(j == 0), stop=(j == 3))
                    if j < 3:
                        mm.then_inc(sq_used, 1)
                mm.then_inc(ps_ready, 1)

            for x, kind in enumerate(("cg", "dq", "dk", "dg")):
                for j in range(4):
                    if (kind, j) == ("dk", 0):
                        layer_norm_sums()
                    if (kind, j) == ("dk", 2):
                        layer_norm_squares()
                    product(("od", kind, j), g0 + 12 + 4 * x + j, hrow, full if kind == "dk" else lat)
            pe.wait_ge(g_ready, G_BASE["od_end"])
            attention("D", TINDEX[("odO", "res", 0)])
            pe.wait_ge(att["D"]["mixed"], QT)
            pe.wait_ge(mix_ready, 4)
            for m in range(KT):
                product(("odO", "res", m), GBASE["odO"] + m,
                        lambda k, c, n: CG[:, k, c:c + n] if k < 4 else DG[:, k - 4, c:c + n], lat)
            norm_sums("n2")
            norm_sums("n3")

            def hg(k, c, n):
                return HG[:, k, c:c + n]

            g0 = GBASE["gla"]
            for m in range(4):
                product(("gla", "k", m), g0 + m, hg, lat, (lambda k: (h_ready, 24 + k + 1)) if m == 0 else None)
            pe.wait_ge(small_in, 32)
            t, o = tile("gla", "glr")
            wait_slot(t)
            for k in range(KT):
                for c, n in lat:
                    mm = pe.matmul(ps[0:16, o + c:o + c + n], GSMALL_Wv[:, k, :], HG[:, k, c:c + n], start=(k == 0), stop=(k == KT - 1))
            mm.then_inc(ps_ready, 1)
            pe.wait_ge(glr_ready, 1)
            for m in range(4):
                t, o = tile("gla", "z", m)
                wait_slot(t)
                for c, n in lat:
                    mm = pe.matmul(ps[:, o + c:o + c + n], GSMALL_2[:, m * P:(m + 1) * P], GLR[0:16, c:c + n], start=True, stop=True)
                mm.then_inc(ps_ready, 1)
                if m % 2 == 0:
                    for i in range(4):
                        wait_weight(g0 + 4 + 2 * m + i)
                for n in range(4 * m, 4 * m + 4):
                    i = n % QT
                    t, o = tile("gla", "v", n)
                    wait_slot(t)
                    for k in range(KT):
                        mm = pe.matmul(ps[:, o:o + 512], HG[:, k, i * P:(i + 1) * P], W[:, :, k, :],
                                       start=(k == 0), stop=(k == KT - 1))
                    mm.then_inc(ps_ready, 1)
            for m in range(4):
                product(("gla", "q", m), g0 + 12 + m, hg, lat)
            for m in range(8):
                product(("gla", "r", m), g0 + 16 + m, hg, lat)
            for h in range(GH):
                pe.wait_ge(kd_ready, h + 1)
                if h:
                    pe.wait_ge(kt_free, h)
                for i in range(QT):
                    mm = pe.transpose(ps[:, TB + i * P:TB + (i + 1) * P], GKT[:, h, i * P:(i + 1) * P], IDENT)
                mm.then_inc(kt_ready, 1)
            tn = TINDEX[("glaN", "ssq", 0)]
            for s in range(2):
                pe.wait_ge(ps_free[s], (tn + 1 - s) // 2)
            pe.wait_ge(kt_free, GH)
            pe.wait_ge(g_ready, G_BASE["gla_end"])
            steps = GH * NCH

            def kv(i):
                h, c = divmod(i, NCH)
                r = 64 * (c % 2)
                if i >= 4:
                    pe.wait_ge(st_ready, i - 3)
                pe.matmul(ps[:, (i % 4) * BANK:(i % 4) * BANK + GDV], GKT[r:r + 64, h, (c // 2) * P:(c // 2 + 1) * P],
                          GV[r:r + 64, c // 2, h * GDV:(h + 1) * GDV], start=True, stop=True).then_inc(kv_ready, 1)

            def chunk_out(i):
                h, c = divmod(i, NCH)
                b = 4 + 2 * (c // 8)
                pe.wait_ge(st_ready, i + 1)
                if c % 8 == 0 and i >= NCH:
                    pe.wait_ge(oe_ready, 2 * (2 * (h - 1) + c // 8) + 2)
                for half in range(2):
                    col = (b + half) * BANK + (c % 8) * CHUNK
                    mm = pe.matmul(ps[:, col:col + CHUNK], STATE[:, i % 2, half * P:(half + 1) * P],
                                   GQT[:, h, c * CHUNK:(c + 1) * CHUNK], start=True, stop=True)
                mm.then_inc(o_ready, 1)

            kv(0)
            kv(1)
            for i in range(steps):
                if i + 2 < steps:
                    kv(i + 2)
                chunk_out(i)
            for h in range(GH):
                t, o = tile("glaN", "ssq", h)
                wait_slot(t)
                for j in range(2):
                    pe.wait_ge(sq_ready, SQ_BASE["glaN"] + 2 * h + j + 1)
                    for c, n in lat:
                        mm = pe.matmul(ps[:, o + c:o + c + n], ONES, S01[:, 0, c:c + n], start=(j == 0), stop=(j == 1))
                    if j == 0:
                        mm.then_inc(sq_used, 1)
                mm.then_inc(ps_ready, 1)
            for m in range(KT):
                product(("glaO", "res", m), GBASE["glaO"] + m, lambda k, c, n: GR[:, k, c:c + n], lat,
                        (lambda k: (gm_ready, k + 1)) if m == 0 else None)
            norm_sums("n4")
            for m in range(UP_T):
                product(("up", "up", m), GBASE["up"] + m, hg, lat, (lambda k: (h_ready, 32 + k + 1)) if m == 0 else None)
            for m in range(KT):
                t, o = tile("down", "res", m)
                pe.wait_ge(down_in[m % 2], 16 * (m // 2 + 1))
                wait_slot(t)
                for k in range(DOWN_K):
                    if m == 0:
                        pe.wait_ge(fm_ready, k + 1)
                    for c, n in lat:
                        mm = pe.matmul(ps[:, o + c:o + c + n], WD[m % 2][:, k, :], ACTV[:, k, c:c + n],
                                       start=(k == 0), stop=(k == DOWN_K - 1))
                mm.then_inc(ps_ready, 1)
            norm_sums("n5")

        @block.scalar
        def _(act):
            count = [0]

            def link(ins):
                count[0] += 1
                ins.then_inc(act_done, 1)
                act.wait_ge(act_done, count[0])

            def ready(ph, kind, i=0):
                t, o = tile(ph, kind, i)
                act.wait_ge(ps_ready, t + 1)
                return t, o

            used = [0]

            def squares(ph):
                for k in range(KT):
                    if ph in X_BASE:
                        act.wait_ge(x_done, X_BASE[ph] + k + 1)
                    if ph == "n3":
                        act.wait_ge(h_ready, 16 + k + 1)
                    if ph == "n0":
                        act.wait_ge(x_in[k // 2], 32)
                    if k >= 3:
                        act.wait_ge(sq_used, SQU_BASE[ph] + k - 2)
                    dst = NSQ(ph, k) if k else NRS(ph)
                    if ph in NORM_CTX:
                        act.activation(dst[:, LAT:TOK], XCv[:, k, :], ACT.Square)
                    act.activation(dst[:, 0:LAT], XL[:, k, :], ACT.Square).then_inc(sq_ready, 1)

            def root(name, i, rs):
                act.wait_ge(ms_ready, MS_BASE[name] + i + 1)
                act.activation(rs, rs, ACT.Sqrt).then_inc(sd_ready, 1)

            def modulate(layer, base):
                for k in range(KT):
                    act.wait_ge(hn, base + k + 1)
                    act.activation(H[:, k, LAT:TOK], H[:, k, LAT:TOK], ACT.Identity, bias=MOD[:, layer, k, 1:2],
                                   scale=MA[:, layer, k, 1:2])
                    act.activation(H[:, k, 0:LAT], H[:, k, 0:LAT], ACT.Identity, bias=MOD[:, layer, k, 0:1],
                                   scale=MA[:, layer, k, 0:1]).then_inc(h_ready, 1)

            act.wait_ge(first_loads, 32)
            act.activation(SC[:, :, :], vcol("c", 0, 16).rearrange("p (k a) -> p k a", a=2), ACT.Silu).then_inc(silu_c, 1)
            squares("n0")
            root("n0", 0, NRS("n0"))
            act.wait_ge(mod_ready, 1)
            modulate(0, 0)

            def even_half(ph, first):
                for m in range(5):
                    t, o = ready(ph, "qk", m)
                    if first:
                        if m >= 2:
                            act.wait_ge(ps_ready, TINDEX[(ph, "ssq", m - 2)] + 1)
                        act.activation(QK[:, m, :], ps[:, o:o + TOK], ACT.Copy)
                        act.activation(SQ[:, m % 2, :], ps[:, o:o + TOK], ACT.Square).then_inc(sq_ready, 1)
                        act.wait_ge(sq_ready, SQ_BASE["evA"] + m + 1)
                        act.nop().then_inc(ps_free[t % 2], 1)
                        if m >= 1:
                            root("evA", m - 1, RS)
                    else:
                        act.activation(QK[:, m, :], ps[:, o:o + TOK], ACT.Copy,
                                       scale=scale_q if m < 4 else 1.0).then_inc(ps_free[t % 2], 1)
                        act.wait_ge(ps_free[t % 2], t // 2 + 1)
                        act.nop().then_inc(raw_ready, 1)
                if first:
                    root("evA", 4, RS)
                for m in range(4):
                    t, o = ready(ph, "gate", m)
                    act.activation(G[:, (0 if first else 4) + m, :], ps[:, o:o + TOK], ACT.Silu).then_inc(ps_free[t % 2], 1)

            def attention(name):
                at = att[name]
                units = at["units"]

                def pad_queries(u):
                    if u >= QP_N:
                        act.wait_ge(at["scores"], u - QP_N + 1)
                    act.activation(*units[u]["pad"], ACT.Copy).then_inc(q_padded, 1)

                if name == "D":
                    act.wait_ge(pads_zeroed, 2)
                    for u in range(3):
                        pad_queries(u)
                for n_st, st in enumerate(at["plan"]):
                    if name == "D" and n_st + 3 < len(units):
                        pad_queries(n_st + 3)
                    if st["X"] is not None:
                        u = st["X"]
                        c0, c1 = units[u]["span"]
                        o = (u % 2) * SLOT
                        act.wait_ge(at["maxed"], u + 1)
                        masked = units[u]["mask"] is not None
                        if u >= 2 and not masked:
                            act.wait_ge(at["t_ready"], tgs(at, u - 2)[-1][0] + 1)
                        src = at["P"][:, u % 2, 0:c1 - c0] if masked else ps[:, o + c0:o + c1]
                        g, h = divmod(u, HEADS)
                        act.activation(at["P"][:, u % 2, 0:c1 - c0], src, ACT.Exp, bias=ST[:, g % 2, 1, h:h + 1],
                                       accum_out=ST[:, g % 2, 2, h:h + 1]).then_inc(at["exped"], 1)
                        if at["sink"] and h == HEADS - 1:
                            act.wait_ge(at["sink_in"], g + 1)
                            act.activation(ST[:, g % 2, 3, :], ST[:, g % 2, 3, :], ACT.Exp).then_inc(at["sink_out"], 1)
                    for tg, u, j, n, eng in st["T"]:
                        if eng == "act":
                            act.wait_ge(at["t_ready"], tg + 1)
                            act.activation(at["PT"][:, u % 2, j * P:(j + n) * P], ps[:, tbank(at, tg):tbank(at, tg) + n * P], ACT.Copy)\
                               .then_inc(tfree(at, tg)[0], 1)

            even_half("evA", True)
            attention("A")
            even_half("evB", False)
            attention("B")
            squares("n1")
            root("n1", 0, NRS("n1"))
            act.wait_ge(mod_ready, 2)
            modulate(1, 8)

            for j in range(4):
                t, o = ready("od", "cgl", j)
                if j:
                    act.wait_ge(u_done, j)
                act.activation(SG, ps[:, o:o + LAT], ACT.Sigmoid).then_inc(sig_ready, 1)
                act.wait_ge(sig_ready, j + 1)
                act.nop().then_inc(ps_free[t % 2], 1)
            def evac(key, dst, n, func=ACT.Copy, scale=1.0):
                t, o = ready(*key)
                act.activation(dst, ps[:, o:o + n], func, scale=scale).then_inc(ps_free[t % 2], 1)
                act.wait_ge(ps_free[t % 2], t // 2 + 1)
                act.nop().then_inc(g_ready, 1)
            for i in range(TOK // P):
                if i == 0:
                    act.wait_ge(u_done, 4)
                evac(("od", "v", i), DV[:, i, :], 512)
            for j in range(4):
                evac(("od", "cg", j), CG[:, j, :], LAT, ACT.Silu)
            for j in range(4):
                evac(("od", "dq", j), DQ[:, j, :], LAT, ACT.Copy, scale_q)
            for j in range(4):
                if j == 2:
                    for i in range(4):
                        act.wait_ge(ln_sub, i + 1)
                        if i:
                            act.wait_ge(sq_used, SQU_BASE["ln"] + i)
                        act.activation(XC[:, 0:LAT], U[:, i, PAD:PAD + LAT], ACT.Square).then_inc(sq_ready, 1)
                evac(("od", "dk", j), DK[:, j, :], TOK)
            root("ln", 0, XC[:, LAT:2 * LAT])
            for j in range(4):
                evac(("od", "dg", j), DG[:, j, :], LAT, ACT.Silu)
                for i in range(4 if j == 1 else 0):
                    act.wait_ge(ln_mul, i + 1)
                    act.activation(U[:, i, PAD:PAD + LAT], U[:, i, PAD:PAD + LAT], ACT.Silu, bias=vcol("ln_b", i),
                                   scale=vcol("ln_g", i)).then_inc(ln_act, 1)
            act.wait_ge(mix_ready, 4)
            attention("D")
            squares("n2")
            root("n2", 0, NRS("n2"))
            squares("n3")
            root("n3", 0, NRS("n3"))

            for m in range(4):
                evac(("gla", "k", m), GKT[:, m, :], LAT)
            t, o = ready("gla", "glr")
            act.activation(GLR[0:16, :], ps[0:16, o:o + LAT], ACT.Copy).then_inc(ps_free[t % 2], 1)
            act.wait_ge(ps_free[t % 2], t // 2 + 1)
            act.nop().then_inc(glr_ready, 1)

            def gate_chain(m):
                act.wait_ge(zb_ready, m + 1)
                link(act.activation(S01[:, 1, :], S01[:, 0, :], ACT.Abs))
                link(act.activation(S01[:, 1, :], S01[:, 1, :], ACT.Exp, scale=-1.0))
                act.activation(S01[:, 1, :], S01[:, 1, :], ACT.Ln, bias=1.0).then_inc(sp_ready, 1)
                act.wait_ge(gc_ready, m + 1)
                act.activation(DEC[:, m, :], S01[:, 0, :].rearrange("p (c s) -> p c s", s=CHUNK)[:, :, CHUNK - 1], ACT.Exp,
                               scale=1.0 / 16)
                act.activation(S01[:, 1, :], S01[:, 1, :], ACT.Exp, scale=1.0 / 16).then_inc(ge_ready, 1)

            for m in range(4):
                gate_chain(m)
                for i in range(4):
                    n = 4 * m + i
                    evac(("gla", "v", n), GV[:, n % QT, (n // QT) * 512:(n // QT + 1) * 512], 512)
            for m in range(4):
                evac(("gla", "q", m), GQT[:, m, :], LAT, ACT.Copy, 128 ** -0.5)
            for m in range(8):
                evac(("gla", "r", m), GR[:, m, :], LAT, ACT.Silu)
            for h in range(GH):
                act.wait_ge(kt_ready, h + 1)
                act.activation(GKT[:, h, :], ps[:, TB:TB + LAT], ACT.Copy).then_inc(kt_free, 1)
            for h in range(GH):
                for c in range(2):
                    act.wait_ge(o_ready, h * NCH + 8 * (c + 1))
                    for half in range(2):
                        b = 4 + 2 * c + half
                        act.activation(HG[:, 2 * h + half, c * 512:(c + 1) * 512], ps[:, b * BANK:(b + 1) * BANK], ACT.Copy)\
                           .then_inc(oe_ready, 1)
            act.wait_ge(oe_ready, 4 * GH)
            for h in range(GH):
                for j in range(2):
                    if j:
                        act.wait_ge(sq_used, SQU_BASE["glaN"] + h + 1)
                    elif h:
                        act.wait_ge(ps_ready, TINDEX[("glaN", "ssq", h - 1)] + 1)
                    act.activation(S01[:, 0, :], HG[:, 2 * h + j, :], ACT.Square).then_inc(sq_ready, 1)
                root("glaN", h, S01[:, 1, :])
            squares("n4")
            root("n4", 0, NRS("n4"))
            for m in range(UP_T):
                t, o = ready("up", "up", m)
                i = up_ffn(m)
                if m >= 4:
                    act.wait_ge(fm_ready, m // 2 - 1)
                act.activation(FACC[:, m % 4, :], ps[:, o:o + LAT], ACT.Identity, bias=vcol("ffn_b", i),
                               scale=vcol("ffn_w", 3 * i + 2)).then_inc(fa_ready, 1)
                if m % 2 == 1:
                    act.wait_ge(fc_ready, m)
                    act.activation(FACC[:, (m - 1) % 4, :], FACC[:, (m - 1) % 4, :], ACT.Silu).then_inc(fs_ready, 1)
            squares("n5")
            root("n5", 0, NRS("n5"))

        @block.vector
        def _(dve):
            count = [0]

            def link(ins):
                count[0] += 1
                ins.then_inc(dve_done, 1)
                dve.wait_ge(dve_done, count[0])

            def ready(ph, kind, i=0):
                t, o = tile(ph, kind, i)
                dve.wait_ge(ps_ready, t + 1)
                return t, o

            def mean_square(name, i, o, t, rs, width, n):
                dve.tensor_scalar(rs, ps[:, o:o + width], 1.0 / n, EPS, ALU.mult, ALU.add).then_inc(ps_free[t % 2], 1)
                dve.wait_ge(ps_free[t % 2], t // 2 + 1)
                dve.engine_nop().then_inc(ms_ready, 1)
                dve.wait_ge(sd_ready, MS_BASE[name] + i + 1)
                link(dve.reciprocal(rs, rs))

            def add_squares(ph, k):
                if k == 0:
                    return
                w = TOK if ph in NORM_CTX else LAT
                dve.wait_ge(sq_ready, SQ_BASE[ph] + k + 1)
                if k >= 2:
                    dve.wait_ge(sq_used, SQU_BASE[ph] + k - 1)
                dve.tensor_tensor(NRS(ph)[:, 0:w], NRS(ph)[:, 0:w], NSQ(ph, k)[:, 0:w], ALU.add).then_inc(sq_used, 1)

            def norm(ph, gain=None, dst=None, meanwhile=None):
                t, o = ready(ph, "nrm")
                full = ph in NORM_CTX
                rs = NRS(ph)
                mean_square(ph, 0, o, t, rs, TOK if full else LAT, D)
                if meanwhile:
                    meanwhile()
                for k in range(KT):
                    if full:
                        dve.tensor_tensor(H[:, k, LAT:TOK], XCv[:, k, :], rs[:, LAT:TOK], ALU.mult)
                        dve.tensor_tensor(H[:, k, 0:LAT], XL[:, k, :], rs[:, 0:LAT], ALU.mult).then_inc(hn, 1)
                    else:
                        dve.scalar_tensor_tensor(dst(k), XL[:, k, :], vcol(gain, k), rs, ALU.mult, ALU.mult).then_inc(h_ready, 1)
                if full:
                    dve.wait_ge(hn, 8 * int(ph[1]) + 8)
                else:
                    dve.wait_ge(h_ready, 8 * int(ph[1]) + 8)

            def finish_mod(layer, n, src):
                mb = vcol("mod_b", 24 * layer, n).unsqueeze(2).to_broadcast([P, n, 2])
                link(dve.tensor_tensor(MOD[:, layer, 0:n, :], src, mb, ALU.add))
                ng = vcol("norm_g", 8 * layer, 8).unsqueeze(2).to_broadcast([P, KT, 2])
                dve.scalar_tensor_tensor(MA[:, layer], MOD[:, layer, 8:16, :], 1.0, ng, ALU.add, ALU.mult).then_inc(mod_ready, 1)

            def first_modulation():
                for q in range(MOD0 // 4):
                    dve.wait_ge(w_mod, 4 * q + 4)
                    dve.tensor_copy(MROW[:, 4 * q * P:4 * (q + 1) * P], mod_rows(4 * q, 4)).then_inc(rows_in_sbuf, 1)
                t, o = ready("mod0", "mod")
                finish_mod(0, MOD0, ps[:, OB:OB + 2 * MOD0].rearrange("p (m a) -> p m a", a=2))
                dve.wait_ge(mod_ready, 1)
                dve.engine_nop().then_inc(ps_free[t % 2], 1)

            dve.wait_ge(first_loads, 32)
            link(dve.tensor_scalar(GQ[:, :], vcol("q_gain"), scale_q, None, ALU.mult))
            for k in range(KT):
                add_squares("n0", k)
            norm("n0", meanwhile=first_modulation)

            n_rope = [0]

            def rope(m):
                if n_rope[0]:
                    dve.wait_ge(qk_done, n_rope[0])
                n_rope[0] += 1
                x = QK[:, m, 0:LAT]
                link(dve.stream_shuffle(SW, x, [i ^ 1 for i in range(32)]))
                link(dve.tensor_tensor(x, x, ROPE[:, 0, :], ALU.mult))
                link(dve.tensor_tensor(SW, SW, ROPE[:, 1, :], ALU.mult))
                dve.tensor_tensor(x, x, SW, ALU.add).then_inc(qk_done, 1)

            def even_half(ph, first):
                if first:
                    dve.wait_ge(rope_in, 16)
                def qknorm(m):
                    t, o = ready(ph, "ssq", m)
                    mean_square("evA", m, o, t, RS, TOK, DH)
                    dve.wait_ge(sq_ready, SQ_BASE["evA"] + m + 1)
                    gain = GQ[:, 0:1] if m < 4 else vcol("k_gain")
                    link(dve.scalar_tensor_tensor(QK[:, m, :], QK[:, m, :], gain, RS, ALU.mult, ALU.mult))
                    rope(m)

                for m in range(5):
                    if first:
                        if m >= 1:
                            qknorm(m - 1)
                    else:
                        dve.wait_ge(raw_ready, m + 1)
                        rope(m)
                for i in range(TOK // P):
                    t, o = ready(ph, "v", i)
                    if not first and i == 0:
                        dve.wait_ge(att["A"]["pv"], 80)
                    dve.tensor_copy(VE[:, i, :], ps[:, o:o + P]).then_inc(ps_free[t % 2], 1)
                    dve.wait_ge(ps_free[t % 2], t // 2 + 1)
                    dve.engine_nop().then_inc(v_ready, 1)
                for m in range(0 if first else 4):
                    dve.wait_ge(w_mod, MOD0 + 2 * m + 2)
                    dve.tensor_tensor(MOD[:, 0, MOD0 + 2 * m:MOD0 + 2 * m + 2, :],
                                      ps[:, TB:TB + 4].rearrange("p (m a) -> p m a", a=2),
                                      vcol("mod_b", MOD0 + 2 * m, 2).unsqueeze(2).to_broadcast([P, 2, 2]), ALU.add)\
                       .then_inc(late_mod_read, 1)
                if first:
                    qknorm(4)

            def attention(name):
                at = att[name]
                units = at["units"]
                for st in at["plan"]:
                    if st["NORM"] is not None:
                        g = st["NORM"]
                        s = g % 2
                        dve.wait_ge(at["pv"], (g + 1) * HEADS)
                        dve.wait_ge(at["exped"], (g + 1) * HEADS)
                        if at["sink"]:
                            dve.wait_ge(at["sink_out"], g + 1)
                            link(dve.tensor_tensor(ST[:, s, 2, :], ST[:, s, 2, :], ST[:, s, 3, :], ALU.add))
                        link(dve.reciprocal(ST[:, s, 2, :], ST[:, s, 2, :]))
                        dve.tensor_tensor(at["ON"].rearrange("p (h d) -> p h d", d=DH),
                                          ps[:, OB:OB + 512].rearrange("p (h d) -> p h d", d=DH),
                                          ST[:, s, 2, :].unsqueeze(2).to_broadcast([P, HEADS, DH]), ALU.mult)\
                           .then_inc(at["normed"], 1)
                    for tg, u, j, n, eng in st["T"]:
                        if eng == "dve":
                            dve.wait_ge(at["t_ready"], tg + 1)
                            dve.tensor_copy(at["PT"][:, u % 2, j * P:(j + n) * P], ps[:, tbank(at, tg):tbank(at, tg) + n * P])\
                               .then_inc(tfree(at, tg)[0], 1)
                    if st["OT"]:
                        tg, g = st["OT"]
                        a, b = units[g * HEADS]["gate"]
                        dve.wait_ge(at["t_ready"], tg + 1)
                        gv = at["gate"](a, b)
                        tb = tbank(at, tg)
                        dve.tensor_tensor(gv, ps[:, tb:tb + 512].rearrange("p (m q) -> p m q", m=4), gv, ALU.mult)\
                           .then_inc(tfree(at, tg)[0], 1)
                        dve.wait_ge(*tfree(at, tg))
                        dve.engine_nop().then_inc(at["mixed"], 1)
                    if st["S"] is not None:
                        u = st["S"]
                        un = units[u]
                        g, h = divmod(u, HEADS)
                        c0, c1 = un["span"]
                        o = (u % 2) * SLOT
                        dve.wait_ge(at["scores"], u + 1)
                        mx, nm = ST[:, g % 2, 0, h:h + 1], ST[:, g % 2, 1, h:h + 1]
                        if un["mask"] is None:
                            if at["sink"]:
                                link(dve.tensor_reduce(mx, ps[:, o + c0:o + c1], AX_X, ALU.max))
                            else:
                                dve.tensor_reduce(nm, ps[:, o + c0:o + c1], AX_X, ALU.max, negate=True).then_inc(at["maxed"], 1)
                        else:
                            pt = at["P"][:, u % 2, 0:c1 - c0]
                            if u >= 2:
                                dve.wait_ge(at["t_ready"], tgs(at, u - 2)[-1][0] + 1)
                            if un["mask"] == "grid":
                                cls = D_CLASS[g]
                                dve.wait_ge(bias_ready, cls * HEADS + h + 1)
                                link(dve.tensor_tensor_reduce(pt[:, 0:D_LOCAL], ps[:, o:o + D_LOCAL],
                                                              BT[:, cls % 2, h * D_LOCAL:(h + 1) * D_LOCAL], 1.0, -3e38,
                                                              ALU.add, ALU.max, mx))
                                link(dve.tensor_tensor_reduce(pt[:, D_LOCAL:D_LOCAL + CTX], ps[:, o + D_LOCAL:o + c1],
                                                              ZERO, 1.0, mx, ALU.add, ALU.max, nm))
                                dve.tensor_scalar(nm, nm, -1.0, None, ALU.mult).then_inc(at["maxed"], 1)
                            else:
                                link(dve.tensor_tensor_reduce(pt, ps[:, o + c0:o + c1], un["mask"], 1.0, -3e38,
                                                              ALU.add, ALU.max, mx))
                        if at["sink"]:
                            dve.scalar_tensor_tensor(nm, mx, -1.0, NSINK[:, h:h + 1], ALU.mult, ALU.min).then_inc(at["maxed"], 1)
                            if h == HEADS - 1:
                                dve.wait_ge(at["maxed"], u + 1)
                                dve.tensor_tensor(ST[:, g % 2, 3, :], ST[:, g % 2, 1, :], vcol("sink", 0, 8), ALU.add)\
                                   .then_inc(at["sink_in"], 1)

            link(dve.tensor_scalar(NSINK[:, :], vcol("sink", 0, 8), -1.0, None, ALU.mult))
            even_half("evA", True)
            attention("A")
            even_half("evB", False)
            dve.wait_ge(bmask_in, 16)
            attention("B")

            def residual(ph, gated, next_norm):
                for m in range(KT):
                    t, o = ready(ph, "res", m)
                    if gated is None:
                        dve.tensor_tensor(XL[:, m, :], ps[:, o:o + LAT], XL[:, m, :], ALU.add).then_inc(ps_free[t % 2], 1)
                    else:
                        if gated == 0:
                            dve.scalar_tensor_tensor(XCv[:, m, :], ps[:, o + LAT:o + TOK], MOD[:, 0, 16 + m, 1:2], XCv[:, m, :],
                                                     ALU.mult, ALU.add)
                        dve.scalar_tensor_tensor(XL[:, m, :], ps[:, o:o + LAT], MOD[:, gated, 16 + m, 0:1], XL[:, m, :],
                                                 ALU.mult, ALU.add).then_inc(ps_free[t % 2], 1)
                    dve.wait_ge(ps_free[t % 2], t // 2 + 1)
                    dve.engine_nop().then_inc(x_done, 1)
                    if m:
                        add_squares(next_norm, m - 1)
                    if ph == "evO":
                        dve.wait_ge(w_mod, MOD0 + 8 + 3 * m + 3)
                        dve.tensor_copy(MODRAW[:, 3 * m:3 * m + 3, :], ps[:, TB:TB + 6].rearrange("p (m a) -> p m a", a=2))\
                           .then_inc(late_mod_read, 1)
                add_squares(next_norm, KT - 1)

            dve.wait_ge(late_mod_read, 4)
            residual("evO", 0, "n1")
            dve.wait_ge(late_mod_read, 4 + KT)
            finish_mod(1, 24, MODRAW[:, :, :])
            norm("n1")
            dve.wait_ge(u_zero, 2)
            for j in range(4):
                t, o = ready("od", "cv", j)
                dve.wait_ge(sig_ready, j + 1)
                dve.tensor_tensor(U[:, j, PAD:PAD + LAT], ps[:, o:o + LAT], SG, ALU.mult).then_inc(ps_free[t % 2], 1)
                dve.wait_ge(ps_free[t % 2], t // 2 + 1)
                dve.engine_nop().then_inc(u_done, 1)
            for j in range(4):
                acc = XC[:, (j % 2) * LAT:(j % 2 + 1) * LAT]
                if j >= 2:
                    dve.wait_ge(conv_done, j - 1)
                w = VOFF["conv_w"] + CONV * j
                link(dve.tensor_scalar(acc, U[:, j, 0:LAT], V[:, w:w + 1], vcol("conv_b", j), ALU.mult, ALU.add))
                for k in range(1, CONV):
                    link(dve.scalar_tensor_tensor(acc, U[:, j, k:k + LAT], V[:, w + k:w + k + 1], acc, ALU.mult, ALU.add))
                dve.tensor_copy(U[:, j, PAD:PAD + LAT], acc).then_inc(conv_done, 1)
            t, o = ready("od", "lnm")
            for j in range(4):
                dve.scalar_tensor_tensor(U[:, j, PAD:PAD + LAT], ps[:, o:o + LAT], -1.0 / 512, U[:, j, PAD:PAD + LAT],
                                         ALU.mult, ALU.add).then_inc(ln_sub, 1)
            dve.wait_ge(ln_sub, 4)
            dve.engine_nop().then_inc(ps_free[t % 2], 1)
            t, o = ready("od", "lnv")
            mean_square("ln", 0, o, t, XC[:, LAT:2 * LAT], LAT, 512)
            for j in range(4):
                dve.tensor_tensor(U[:, j, PAD:PAD + LAT], U[:, j, PAD:PAD + LAT], XC[:, LAT:2 * LAT], ALU.mult).then_inc(ln_mul, 1)
            for j in range(4):
                dve.wait_ge(ln_act, j + 1)
                dve.wait_ge(g_ready, G_BASE["cg"] + j + 1)
                dve.tensor_tensor(CG[:, j, :], CG[:, j, :], U[:, j, PAD:PAD + LAT], ALU.mult).then_inc(mix_ready, 1)
            dve.wait_ge(mix_ready, 4)
            dve.wait_ge(g_ready, G_BASE["od_end"])
            link(dve.memset(ZERO, 0.0))
            attention("D")
            residual("odO", 1, "n2")
            norm("n2", "final_g", lambda k: XL[:, k, :])
            for k in range(KT):
                add_squares("n3", k)
            norm("n3", "mix_g", lambda k: HG[:, k, :])

            dve.wait_ge(pool_done, 7)
            for m in range(4):
                t, o = ready("gla", "z", m)
                if m:
                    dve.wait_ge(kd_ready, m)
                link(dve.tensor_scalar(S01[:, 0, :], ps[:, o:o + LAT], vcol("gate_b", m), None, ALU.add))
                dve.engine_nop().then_inc(ps_free[t % 2], 1)
                dve.engine_nop().then_inc(zb_ready, 1)
                dve.wait_ge(sp_ready, m + 1)
                link(dve.scalar_tensor_tensor(S01[:, 1, :], S01[:, 0, :], 0.0, S01[:, 1, :], ALU.min, ALU.subtract))
                link(dve.tensor_tensor_scan(S01[:, 0, :], SMASK, S01[:, 1, :], 0.0, ALU.mult, ALU.add))
                gs = S01[:, 0, :].rearrange("p (c s) -> p c s", s=CHUNK)
                dve.tensor_tensor(S01[:, 1, :].rearrange("p (c s) -> p c s", s=CHUNK),
                                  gs[:, :, CHUNK - 1:CHUNK].to_broadcast([P, NCH, CHUNK]), gs, ALU.subtract).then_inc(gc_ready, 1)
                dve.wait_ge(ge_ready, m + 1)
                dve.wait_ge(g_ready, G_BASE["od_end"] + m + 1)
                dve.tensor_tensor(GKT[:, m, :], GKT[:, m, :], S01[:, 1, :], ALU.mult).then_inc(kd_ready, 1)
            for i in range(GH * NCH):
                h, c = divmod(i, NCH)
                dve.wait_ge(kv_ready, i + 1)
                if i >= 2:
                    dve.wait_ge(o_ready, i - 1)
                if i:
                    dve.wait_ge(st_ready, i)
                kv = ps[:, (i % 4) * BANK:(i % 4) * BANK + GDV]
                if c == 0:
                    dve.tensor_copy(STATE[:, i % 2, :], kv).then_inc(st_ready, 1)
                else:
                    dve.scalar_tensor_tensor(STATE[:, i % 2, :], STATE[:, (i - 1) % 2, :], DEC[:, h, c:c + 1], kv,
                                             ALU.mult, ALU.add).then_inc(st_ready, 1)
            for h in range(GH):
                t, o = ready("glaN", "ssq", h)
                if h:
                    dve.wait_ge(gm_ready, 2 * h)
                mean_square("glaN", h, o, t, S01[:, 1, :], LAT, GDV)
                for j in range(2):
                    x = HG[:, 2 * h + j, :]
                    link(dve.scalar_tensor_tensor(x, x, vcol("gla_g", 2 * h + j), S01[:, 1, :], ALU.mult, ALU.mult))
                    dve.tensor_tensor(GR[:, 2 * h + j, :], GR[:, 2 * h + j, :], x, ALU.mult).then_inc(gm_ready, 1)
            residual("glaO", None, "n4")
            norm("n4", "ffn_g", lambda k: HG[:, k, :])
            for m in range(UP_T):
                t, o = tile("up", "up", m)
                i = up_ffn(m)
                dve.wait_ge(fa_ready, m + 1)
                link(dve.scalar_tensor_tensor(FACC[:, m % 4, 1:LAT], ps[:, o:o + LAT - 1], vcol("ffn_w", 3 * i + 1),
                                              FACC[:, m % 4, 1:LAT], ALU.mult, ALU.add))
                dve.scalar_tensor_tensor(FACC[:, m % 4, 2:LAT], ps[:, o:o + LAT - 2], vcol("ffn_w", 3 * i),
                                         FACC[:, m % 4, 2:LAT], ALU.mult, ALU.add).then_inc(fc_ready, 1)
                dve.wait_ge(fc_ready, m + 1)
                dve.engine_nop().then_inc(ps_free[t % 2], 1)
                if m % 2 == 1:
                    dve.wait_ge(fs_ready, m // 2 + 1)
                    dve.tensor_tensor(ACTV[:, m // 2, :], FACC[:, (m - 1) % 4, :], FACC[:, m % 4, :], ALU.mult).then_inc(fm_ready, 1)
            residual("down", None, "n5")
            norm("n5", "out_g", lambda k: XL[:, k, :])


def kernel(**inputs):
    import numpy as np
    import concourse.bacc as bacc
    from concourse.bass_utils import run_bass_kernel_spmd as run

    x = {k: np.asarray(v) for k, v in inputs.items()}

    def tiles(w):
        k, m = w.shape
        return w.reshape(k // P, P, m // P, P).transpose(2, 1, 0, 3).reshape(m // P, P, k)

    def cols(v):
        return v.reshape(-1, P).T

    even = x["ev_w_in"][0]
    parts = {}
    at = 0
    for name, width in (("aq", 512), ("ak", 128), ("av", 128), ("ag", 512), ("bq", 512), ("bk", 128), ("bv", 128), ("bg", 512)):
        parts[name] = even[:, at:at + width]
        at += width
    order = np.concatenate([np.arange(h * DH, (h + 1) * DH) for t in range(4) for h in (t, t + 4)])
    ev = {s: np.concatenate([parts[s + "q"][:, order], parts[s + "k"], parts[s + "v"], parts[s + "g"]], axis=1) for s in "ab"}
    od = tiles(x["od_w_in"][0])
    cv, cgl, cg, dq, dk, dv, dg = (od[4 * i:4 * i + 4] for i in range(7))
    gla = tiles(x["gla_w_in_2"][0][:, :3072])
    up = tiles(x["ffn_w_up_2"][0])
    mod0, evb = tiles(x["mod_w"][0]), tiles(ev["b"])
    wall = np.concatenate([
        mod0[:MOD0], tiles(ev["a"]), evb[:6],
        np.concatenate([evb[6:, None], mod0[MOD0:].reshape(4, 2, P, D)], axis=1).reshape(-1, P, D),
        np.concatenate([tiles(x["ev_w_out"][0])[:, None], tiles(x["mod_w"][1]).reshape(KT, 3, P, D)], axis=1).reshape(-1, P, D),
        np.stack([t for pair in zip(cgl, cv) for t in pair]), dv, cg, dq, dk, dg, tiles(x["od_w_out"][0]),
        gla[4:8], gla[8:16], gla[0:4], gla[16:24], tiles(x["gla_w_out_2"][0]),
        np.stack([t for pair in zip(up[:DOWN_K], up[DOWN_K:]) for t in pair])])
    wdown = tiles(x["ffn_w_down_2"][0])
    wglr = x["gla_w_in_2"][0][:, 3072:].reshape(KT, P, 16).transpose(1, 0, 2).reshape(P, KT * 16)
    vec = np.concatenate([
        np.stack([cols(x["c"][0]), cols(x["c_ctx"])], axis=2).reshape(P, 16),
        cols(x["mod_b"].reshape(-1)), cols(x["norm_g"].reshape(-1)),
        np.tile(x["a_q_gain"][0], 2)[:, None], np.tile(x["a_k_gain"][0], 2)[:, None],
        np.broadcast_to(x["b_sink"][0][None], (P, 8)),
        x["c_dw_w"][0].reshape(CONV, 4, P).transpose(2, 1, 0).reshape(P, 4 * CONV), cols(x["c_dw_b"][0]),
        cols(x["c_ln_g"][0]), cols(x["c_ln_b"][0]), cols(x["final_g"]), cols(x["mix_norm_w_2"][0]),
        cols(x["ffn_norm_w_2"][0]), cols(x["final_norm_w_2"]), cols(x["gla_b_gate_2"][0]), cols(x["gla_norm_w_2"][0]),
        x["ffn_conv_w_2"][0].reshape(3, UP_T, P).transpose(2, 1, 0).reshape(P, 3 * UP_T), cols(x["ffn_conv_b_2"][0])], axis=1)

    def feature_major(a):
        return a[0].T.reshape(KT, P, -1).transpose(1, 0, 2)

    f = np.float32
    consts = np.concatenate([np.eye(P), np.ones((P, P)), np.kron(np.eye(2), np.ones((64, 64)))], axis=1).astype(f)
    pos = np.arange(LAT)
    freqs = (f(10000.0) ** (-np.arange(0, DH // 2, 2, dtype=f) / f(DH // 2))).astype(f)
    ang = np.concatenate([(pos // GRID).astype(f)[:, None] * freqs, (pos % GRID).astype(f)[:, None] * freqs], axis=1)
    pair = (np.arange(P) % DH) // 2
    sign = np.where(np.arange(P) % 2 == 0, -1.0, 1.0)[:, None]
    ropes = np.stack([np.cos(ang).T[pair], np.sin(ang).T[pair] * sign], axis=1).astype(f)
    p, c = np.arange(P)[:, None], np.arange(384)[None]
    band = np.where((c >= p) & (c <= p + 256), 0.0, -1e30)
    zero = np.zeros((P, CTX))
    bmask = np.concatenate([band, zero, band[:, :256], zero], axis=1).astype(f)
    dmask = np.zeros((5, P, 10, GRID), f)
    cs = np.clip(np.arange(GRID) - 8, 0, GRID - 16)[:, None]
    kc = np.arange(GRID)[None]
    in_cols = (kc >= cs) & (kc < cs + 16)
    for cls in range(5):
        qt = D_CLASS.index(cls)
        for half in range(2):
            rs = min(max(2 * qt + half - 4, 0), 8)
            for i in range(10):
                row_in = rs <= D_BASE[qt] + i < rs + 8
                dmask[cls, 64 * half:64 * half + 64, i] = np.where(in_cols & row_in, 0.0, -1e30)
    dmask = dmask.reshape(5, P, D_LOCAL)
    rpb = np.zeros((8, RPB_ROWS, 31), f)
    rpb[:, 2:17] = x["d_rpb"][0]
    rpb = np.pad(rpb.reshape(1, -1), ((0, 0), (RPB_PAD, RPB_PAD)))

    arrays = {"wall": wall, "wdown": wdown, "wglr": wglr, "wgate2": x["gla_w_gate2_2"][0], "vec": vec,
              "xl_in": feature_major(x["x"]), "xc_in": feature_major(x["ctx"]), "consts": consts, "ropes": ropes,
              "bmask": bmask, "dmask": dmask, "rpb": rpb}
    arrays = {k: np.ascontiguousarray(v) for k, v in arrays.items()}
    nc = bacc.Bacc("TRN2", target_bir_lowering=False, num_devices=1)
    args = {k: nc.dram_tensor(f"in_{k}", v.shape, F32, kind="ExternalInput").ap() for k, v in arrays.items()}
    out = nc.dram_tensor("out", (P, KT, LAT), F32, kind="ExternalOutput").ap()
    program(nc, **args, out=out)
    got = run(nc, [{f"in_{k}": v for k, v in arrays.items()}], core_ids=[0]).results[0]["out"]
    return got.transpose(1, 0, 2).reshape(D, LAT).T[None]
```
